# Optimizing a Trainium2 kernel written in Bass

```python
import math
import jax, jax.numpy as jnp
from jax import lax
import numpy as np

D_MODEL = 1024
BATCH = 1
SEQ = 2048
DEPTH = 1
DEC_BATCH = 1
DEC_SEQ = 32
PAST_LEN = 512

CHUNK = 64
N_META = 16
D_LRU = 1024
LRU_HEADS = 8
LRU_BLOCK = D_LRU // LRU_HEADS
LRU_C = 8.0
CONV_W = 4
D_POOL = 1024
POOL_WINDOWS = (2, 4, 8, 16)
POOL_GROUPS = len(POOL_WINDOWS)
POOL_GROUP = D_POOL // POOL_GROUPS
POOL_MAX = 16
D_FF = ((8 * D_MODEL // 3 + 255) // 256) * 256
D_IN = D_LRU + D_POOL + 2 * D_MODEL
EPS = 1e-6

kernel_name = 'hawk_pool_hybrid_stream_step'

def _rmsnorm(x, g):
    x32 = x.astype(jnp.float32)
    y = x32 * lax.rsqrt(jnp.mean(x32 * x32, axis=-1, keepdims=True) + EPS)
    return (y * g.astype(jnp.float32)).astype(x.dtype)

def _causal_conv(x, prev, w, b):
    T = x.shape[1]
    xe = jnp.concatenate([prev, x], axis=1)
    y = b + w[0] * xe[:, 0:T]
    for k in range(1, CONV_W):
        y = y + w[k] * xe[:, k:k + T]
    return y, xe[:, -(CONV_W - 1):]

def _lin_combine(left, right):
    a_l, b_l = left
    a_r, b_r = right
    return a_l * a_r, a_r * b_l + b_r

def _rg_lru(x, pos, h0, w_r, b_r, w_i, b_i, lam):
    B, T, C = x.shape
    xh = x.reshape(B, T, LRU_HEADS, LRU_BLOCK)
    r = jax.nn.sigmoid(jnp.einsum('bthi,hij->bthj', xh, w_r).reshape(B, T, C) + b_r)
    i = jax.nn.sigmoid(jnp.einsum('bthi,hij->bthj', xh, w_i).reshape(B, T, C) + b_i)
    log_a = LRU_C * r.astype(jnp.float32) * jax.nn.log_sigmoid(lam.astype(jnp.float32))
    a = jnp.exp(log_a)
    mult = jnp.sqrt(-jnp.expm1(2.0 * log_a))
    mult = jnp.where((pos == 0)[None, :, None], 1.0, mult)
    bt = mult * (i * x).astype(jnp.float32)
    bt = bt.at[:, 0].add(a[:, 0] * h0.astype(jnp.float32))
    _, h = lax.associative_scan(_lin_combine, (a, bt), axis=1)
    return h.astype(x.dtype), h[:, -1].astype(x.dtype)

def _pool_mix(x, pos, prev, w_g, scale):
    B, T, C = x.shape
    P = POOL_MAX - 1
    xe_raw = jnp.concatenate([prev, x], axis=1)
    xe = xe_raw.astype(jnp.float32)
    cs = jnp.cumsum(xe, axis=1)
    cs = jnp.concatenate([jnp.zeros_like(cs[:, :1]), cs], axis=1)
    outs = []
    for g, w in enumerate(POOL_WINDOWS):
        lo, hi = g * POOL_GROUP, (g + 1) * POOL_GROUP
        s = cs[:, P + 1:P + 1 + T, lo:hi] - cs[:, P + 1 - w:P + 1 - w + T, lo:hi]
        cnt = jnp.minimum(w, pos + 1).astype(jnp.float32)[None, :, None]
        outs.append(s / cnt)
    pooled = jnp.concatenate(outs, axis=-1)
    d = (pooled - xe[:, P:]).astype(x.dtype).reshape(B, T, POOL_GROUPS, POOL_GROUP)
    y = jnp.einsum('btgi,gij->btgj', d, w_g).reshape(B, T, C) * scale
    return y, xe_raw[:, -P:]

def _mixer(xn, pos, conv_prev, h0, pool_prev, w_in, conv_w, conv_b, w_r, b_r, w_i, b_i,
           lam, pool_w, pool_scale, w_br_a, w_br_b, w_out):
    proj = xn @ w_in
    x_a, x_b, g_a, g_b = jnp.split(proj, [D_LRU, D_LRU + D_POOL, D_LRU + D_POOL + D_MODEL], axis=-1)
    c_a, conv_state = _causal_conv(x_a, conv_prev, conv_w, conv_b)
    y_a, h_last = _rg_lru(c_a, pos, h0, w_r, b_r, w_i, b_i, lam)
    y_b, pool_state = _pool_mix(x_b, pos, pool_prev, pool_w, pool_scale)
    merged = jax.nn.sigmoid(g_a) * (y_a @ w_br_a) + jax.nn.sigmoid(g_b) * (y_b @ w_br_b)
    return merged @ w_out, conv_state, h_last, pool_state

def _swiglu(xn, w_gu, w_down):
    gu = xn @ w_gu
    g, u = jnp.split(gu, [D_FF], axis=-1)
    return (jax.nn.silu(g) * u) @ w_down

def setup_inputs(seed: int = 0) -> dict:
    key = jax.random.key(seed)
    ks = jax.random.split(key, 26)
    f32 = jnp.float32
    nrm = lambda k, s, sc: jax.random.normal(k, s, f32) * sc
    u = jax.random.uniform(ks[10], (DEPTH, D_LRU), f32, 0.9, 0.999)
    a_base = u ** (1.0 / LRU_C)
    lam = jnp.log(a_base) - jnp.log1p(-a_base)
    return {
        'x_prompt': nrm(ks[0], (BATCH, SEQ, D_MODEL), 1.0),
        'x_sample': nrm(ks[1], (DEC_BATCH, DEC_SEQ, D_MODEL), 1.0),
        'state_conv': nrm(ks[2], (DEPTH, DEC_BATCH, CONV_W - 1, D_LRU), 1.0),
        'state_lru': nrm(ks[3], (DEPTH, DEC_BATCH, D_LRU), 0.5),
        'state_pool': nrm(ks[4], (DEPTH, DEC_BATCH, POOL_MAX - 1, D_POOL), 1.0),
        'meta_tokens': nrm(ks[5], (N_META, D_MODEL), 1.0),
        'norm1_g': 1.0 + nrm(ks[6], (DEPTH, D_MODEL), 0.05),
        'w_in': nrm(ks[7], (DEPTH, D_MODEL, D_IN), D_MODEL ** -0.5),
        'conv_w': nrm(ks[8], (DEPTH, CONV_W, D_LRU), CONV_W ** -0.5),
        'conv_b': nrm(ks[9], (DEPTH, D_LRU), 0.01),
        'lam': lam,
        'w_r': nrm(ks[11], (DEPTH, LRU_HEADS, LRU_BLOCK, LRU_BLOCK), LRU_BLOCK ** -0.5),
        'b_r': nrm(ks[12], (DEPTH, D_LRU), 0.01),
        'w_i': nrm(ks[13], (DEPTH, LRU_HEADS, LRU_BLOCK, LRU_BLOCK), LRU_BLOCK ** -0.5),
        'b_i': nrm(ks[14], (DEPTH, D_LRU), 0.01),
        'pool_w': nrm(ks[15], (DEPTH, POOL_GROUPS, POOL_GROUP, POOL_GROUP), POOL_GROUP ** -0.5),
        'pool_scale': 1.0 + nrm(ks[16], (DEPTH, D_POOL), 0.05),
        'w_br_a': nrm(ks[17], (DEPTH, D_LRU, D_MODEL), D_LRU ** -0.5),
        'w_br_b': nrm(ks[18], (DEPTH, D_POOL, D_MODEL), D_POOL ** -0.5),
        'w_out': nrm(ks[19], (DEPTH, D_MODEL, D_MODEL), D_MODEL ** -0.5),
        'norm2_g': 1.0 + nrm(ks[20], (DEPTH, D_MODEL), 0.05),
        'w_gu': nrm(ks[21], (DEPTH, D_MODEL, 2 * D_FF), D_MODEL ** -0.5),
        'w_down': nrm(ks[22], (DEPTH, D_FF, D_MODEL), D_FF ** -0.5),
        'final_g': 1.0 + nrm(ks[23], (D_MODEL,), 0.05),
    }

def reference(x_prompt, x_sample, state_conv, state_lru, state_pool, meta_tokens,
              norm1_g, w_in, conv_w, conv_b, lam, w_r, b_r, w_i, b_i, pool_w, pool_scale,
              w_br_a, w_br_b, w_out, norm2_g, w_gu, w_down, final_g):
    B = x_prompt.shape[0]
    meta = jnp.broadcast_to(meta_tokens[None].astype(x_prompt.dtype), (B, N_META, D_MODEL))
    xp = jnp.concatenate([meta, x_prompt], axis=1)
    xs = x_sample
    Tp, Ts = xp.shape[1], xs.shape[1]
    pos_p = jnp.arange(Tp, dtype=jnp.int32)
    pos_s = PAST_LEN + jnp.arange(Ts, dtype=jnp.int32)
    zconv = jnp.zeros((B, CONV_W - 1, D_LRU), xp.dtype)
    zh = jnp.zeros((B, D_LRU), xp.dtype)
    zpool = jnp.zeros((B, POOL_MAX - 1, D_POOL), xp.dtype)
    cp_l, hp_l, pp_l, cs_l, hs_l, ps_l = [], [], [], [], [], []
    for l in range(DEPTH):
        lw = (w_in[l], conv_w[l], conv_b[l], w_r[l], b_r[l], w_i[l], b_i[l], lam[l],
              pool_w[l], pool_scale[l], w_br_a[l], w_br_b[l], w_out[l])
        mp, c_p, h_p, p_p = _mixer(_rmsnorm(xp, norm1_g[l]), pos_p, zconv, zh, zpool, *lw)
        ms, c_s, h_s, p_s = _mixer(_rmsnorm(xs, norm1_g[l]), pos_s, state_conv[l], state_lru[l],
                                   state_pool[l], *lw)
        xp = xp + mp
        xs = xs + ms
        xp = xp + _swiglu(_rmsnorm(xp, norm2_g[l]), w_gu[l], w_down[l])
        xs = xs + _swiglu(_rmsnorm(xs, norm2_g[l]), w_gu[l], w_down[l])
        cp_l.append(c_p); hp_l.append(h_p); pp_l.append(p_p)
        cs_l.append(c_s); hs_l.append(h_s); ps_l.append(p_s)
    y_prompt = _rmsnorm(xp, final_g)[:, N_META:]
    y_sample = _rmsnorm(xs, final_g)
    return (y_prompt, y_sample, jnp.stack(cp_l), jnp.stack(hp_l), jnp.stack(pp_l),
            jnp.stack(cs_l), jnp.stack(hs_l), jnp.stack(ps_l))


_drawn_inputs = setup_inputs


def setup_inputs(seed=0):
    import zlib

    import numpy as np

    out = dict(_drawn_inputs(seed))
    spreads = {}
    factors = {'b_r': 24.251, 'b_i': 8.0}
    for name, (base, spread) in spreads.items():
        noise = np.random.default_rng([zlib.crc32(name.encode()), seed]).standard_normal(out[name].shape)
        drawn = base * np.exp(spread * noise) if base else spread * noise
        out[name] = __import__('jax').numpy.asarray(drawn.astype(out[name].dtype))
    for name, factor in factors.items():
        out[name] = (out[name] * factor).astype(out[name].dtype)
    return out
```

```python
import numpy as np
import concourse.bass as bass
from concourse import mybir
from contextlib import ExitStack

P = 128
D = 1024
KT = D // P
SEQ, META, DEC, PAST = 2048, 16, 32, 512
NB = 3
CH = 2
PTOK = (SEQ + META) // NB
STOK = -(-DEC // NB)
SCOL = STOK + 1
PC, SC = PTOK // CH, SCOL // CH
CW = PC + SC
B = CH * CW
CONV = 4
TC = PTOK + (CONV - 1) + SCOL + 1
WINDOWS = (2, 4, 8, 16)
PH = 15
TP = PH + PTOK + PH + SCOL
TW = 732
FF = 2816
FT = FF // P
PAIRS = FT // 2
EPS = 1e-6
LRU_C = 8.0
G1, CW0, CB, BR, BI, LAM, PSC, G2, GF = 0, 1, 5, 6, 7, 8, 9, 10, 11
NCST = 12
S_CONV, S_LRU, S_POOL, NST = 0, 8, 12, 44
XORDER = [2, 3, 4, 5, 6, 7, 0, 1]
SLOT_XA, SLOT_GA, SLOT_A, SLOT_WIN, SLOT_B, SLOT_O, SLOT_MLP = 0, 8, 16, 24, 40, 48, 56
NSLOT = SLOT_MLP + 6 * PAIRS
USE = (61, 61, 45, 48)
TILES = 215


def tile_xa(b, h):
    return b * TILES + h + 1


def tile_gate(b, h):
    return b * TILES + h * 3 + 9


def tile_a(b, m):
    return b * TILES + m + 33


def tile_window(b, g):
    return b * TILES + g * 6 + 41


def tile_b(b, m):
    return b * TILES + m + 65


def tile_o(b, m):
    return b * TILES + m + 73


def tile_norm2(b):
    return b * TILES + 81


def tile_mlp(b, i):
    return b * TILES + i * 12 + 82


def gate_use(b, q, h):
    return b * USE[2 + q] + h + q


def mlp_use(b, g, i):
    return b * USE[g] + i * 3 + (28, 28, 12, 14)[g]


def wsums(b, g, j):
    return b * 20 + 2 * (g * (g + 1) // 2) + j * (g + 1)


def build(nc, dx, dwm, dws, dcst, dfix, dst0, dy, dst):
    f32 = mybir.dt.float32
    f32r = mybir.dt.float32r
    ALU = mybir.AluOpType
    ACT = mybir.ActivationFunctionType
    MUL, ADD, SUB = ALU.mult, ALU.add, ALU.subtract
    ctx = ExitStack()
    with ctx:
        def sb(name, shape, dt=f32):
            return ctx.enter_context(nc.sbuf_tensor(name, shape, dt))

        def sem(name):
            return ctx.enter_context(nc.semaphore(name))

        xhi, xlo = sb("xhi", [P, KT, B], f32r), sb("xlo", [P, KT, B], f32r)
        yhi, ylo = sb("yhi", [P, KT, TC], f32r), sb("ylo", [P, KT, TC], f32r)
        main = sb("main", [P, KT, B])
        gate = sb("gate", [P, KT, TC])
        wraw = sb("wraw", [P, 2, KT * P])
        whi, wlo = sb("whi", [P, 2, KT, P], f32r), sb("wlo", [P, 2, KT, P], f32r)
        sraw = sb("sraw", [P, 4 * P])
        shi, slo = sb("shi", [P, 4, P], f32r), sb("slo", [P, 4, P], f32r)
        rstd = sb("rstd", [P, 2, B])
        tmp = sb("tmp", [P, 8, TW])
        tbuf = sb("tbuf", [P, 2, TW])
        xin = sb("xin", [P, 2, B])
        state = sb("state", [P, KT, NST])
        cst = sb("cst", [P, NCST, KT])
        lac = sb("lac", [P, 8, KT])
        fix = sb("fix", [P, 66])
        ones = sb("ones", [P, P])
        epsc = sb("epsc", [P, 1])
        credit = sb("credit", [P, 8])
        ps = ctx.enter_context(nc.psum_tensor("ps", [P, 4, CH, 512], f32))

        consts_in = sem("consts_in")
        x_in = [sem("x_in0"), sem("x_in1")]
        main_in = [sem("main_in0"), sem("main_in1")]
        side_in = sem("side_in")
        y_stored = sem("y_stored")
        state_stored = sem("state_stored")
        main_hi, main_split, main_begun = sem("main_hi"), sem("main_split"), sem("main_begun")
        side_hi, side_split = sem("side_hi"), sem("side_split")
        ready = sem("psum_ready")
        drained = [sem(f"psum_drained{g}") for g in range(4)]
        setup = sem("setup")
        lam_exp, lam_chain, lam_done = sem("lam_exp"), sem("lam_chain"), sem("lam_done")
        xg_hi, xg_lo, x_sq, q1_zero, q1_sum, rstd1 = (sem(n) for n in ("xg_hi", "xg_lo", "x_sq", "q1_zero", "q1_sum", "rstd1"))
        xa_hist, xa_part, xa_saved, tap3, tap, c_hi, c_lo = (sem(n) for n in ("xa_hist", "xa_part", "xa_saved", "tap3", "tap", "c_hi", "c_lo"))
        tanh_done, a_done, mult_done, ix_done, a2_done, q_done = (sem(n) for n in ("tanh_done", "a_done", "mult_done", "ix_done", "a2_done", "q_done"))
        pos0, bt_done, scan_p, scan_s, h_saved, ya_hi, ya_lo, sig_a = (sem(n) for n in ("pos0", "bt_done", "scan_p", "scan_s", "h_saved", "ya_hi", "ya_lo", "sig_a"))
        xb_hist, xb_part, xb_saved, wsum, wfix, d_done, d_hi, d_lo, yb_hi, sig_b = (sem(n) for n in (
            "xb_hist", "xb_part", "xb_saved", "wsum", "wfix", "d_done", "d_hi", "d_lo", "yb_hi", "sig_b"))
        merged, m_hi, m_lo = sem("merged"), sem("m_hi"), sem("m_lo")
        x1_hi, x1_lo, x1_sq, q2_zero, q2_sum, rstd2 = (sem(n) for n in ("x1_hi", "x1_lo", "x1_sq", "q2_zero", "q2_sum", "rstd2"))
        silu, sr_done, h_hi, h_lo = sem("silu"), sem("sr_done"), sem("h_hi"), sem("h_lo")
        x2_sq, q3_zero, q3_sum, rstd3, y_done, unfix = (sem(n) for n in ("x2_sq", "q3_zero", "q3_sum", "rstd3", "y_done", "unfix"))

        block = ctx.enter_context(nc.Block())

        def bank(g, c0, c1):
            return ps[:, g, :, c0:c1]

        def two(ap):
            return ap.rearrange("p (c n) -> p c n", c=CH)

        def prompt(t):
            return two(t)[:, :, 0:PC]

        def sample(t):
            return two(t)[:, :, PC:CW]

        @block.sync
        def _(sp):
            for dst_, src_ in ((cst, dcst), (fix, dfix), (state, dst0)):
                sp.dma_start(dst_[:], src_).then_inc(consts_in, 16)

            def load_main(b, pos, par):
                sp.wait_ge(main_split, b * NSLOT + pos + 1)
                sp.nop(nofuse=True)
                sp.dma_start(wraw[:, par, :], dwm[pos]).then_inc(main_in[par], 16)

            def load_side(b, s, width):
                sp.wait_ge(side_split, b * 12 + s + 1)
                sp.nop(nofuse=True)
                sp.dma_start(sraw[:, 0:width], dws[s, :, 0:width]).then_inc(side_in, 16)

            def block_loads(b, last):
                load_main(b, 1, 1)
                with sp.Fori(0, 3) as i:
                    load_main(b, SLOT_XA + 2 + i * 2, 0)
                    load_main(b, SLOT_XA + 3 + i * 2, 1)
                with sp.Fori(0, 4) as i:
                    for j in range(2):
                        load_side(b, i * 2 + j, 2 * P)
                        load_main(b, SLOT_GA + j + i * 2, j)
                with sp.Fori(0, 4) as i:
                    for j in range(2):
                        load_main(b, SLOT_A + j + i * 2, j)
                with sp.Fori(0, 4) as g:
                    load_main(b, SLOT_WIN + g * 4, 0)
                    load_main(b, SLOT_WIN + 1 + g * 4, 1)
                    load_side(b, g + 8, 4 * P)
                    load_main(b, SLOT_WIN + 2 + g * 4, 0)
                    load_main(b, SLOT_WIN + 3 + g * 4, 1)
                with sp.Fori(0, (NSLOT - SLOT_B) // 2) as i:
                    for j in range(2):
                        load_main(b, SLOT_B + j + i * 2, j)
                if not last:
                    sp.wait_ge(main_split, (b + 1) * NSLOT + 1)
                    sp.nop(nofuse=True)
                    sp.dma_start(wraw[:, 0, :], dwm[0]).then_inc(main_in[0], 16)

            sp.wait_ge(setup, 1)
            load_main(0, 0, 0)
            with sp.Fori(0, NB - 1) as b:
                block_loads(b, False)
            block_loads(NB - 1, True)
            sp.wait_ge(h_saved, 8 * NB)
            sp.wait_ge(xb_saved, 16 * NB)
            sp.dma_start(dst, state[:]).then_inc(state_stored, 16)
            sp.wait_ge(state_stored, 16)
            sp.wait_ge(y_stored, 16 + 16 * KT * NB)

        @block.gpsimd
        def _(pool):
            def split_main(b, pos, half, par):
                n = b * NSLOT + pos
                pool.wait_ge(main_in[par], (b * (NSLOT // 2) + half + 1) * 16)
                pool.nop(nofuse=True)
                pool.wait_ge(main_begun, n + 1)
                pool.nop(nofuse=True)
                nc.gpsimd.tensor_copy(whi[:, par].rearrange("p k c -> p (k c)"), wraw[:, par, :]).then_inc(main_hi, 1)
                pool.wait_ge(main_hi, n + 1)
                pool.nop(nofuse=True)
                nc.gpsimd.tensor_tensor(wlo[:, par].rearrange("p k c -> p (k c)"), wraw[:, par, :],
                                        whi[:, par].rearrange("p k c -> p (k c)").bitcast(f32), SUB).then_inc(main_split, 1)

            def split_pair(b, first, i, step=2):
                for j in range(2):
                    split_main(b, i * step + (first + j), i * (step // 2) + first // 2, j)

            def split_side(b, s, tiles, free):
                n = b * 12 + s
                pool.wait_ge(side_in, (n + 1) * 16)
                pool.nop(nofuse=True)
                pool.wait_ge(ready, free)
                pool.nop(nofuse=True)
                w = tiles * P
                hi2, lo2 = shi[:, :, :].rearrange("p k c -> p (k c)"), slo[:, :, :].rearrange("p k c -> p (k c)")
                nc.gpsimd.tensor_copy(hi2[:, 0:w], sraw[:, 0:w]).then_inc(side_hi, 1)
                pool.wait_ge(side_hi, n + 1)
                pool.nop(nofuse=True)
                nc.gpsimd.tensor_tensor(lo2[:, 0:w], sraw[:, 0:w], hi2[:, 0:w].bitcast(f32), SUB).then_inc(side_split, 1)

            def block_split(b, last):
                split_main(b, 1, 0, 1)
                with pool.Fori(0, 3) as i:
                    split_pair(b, SLOT_XA + 2, i)
                with pool.Fori(0, 4) as i:
                    for j in range(2):
                        split_side(b, i * 2 + j, 2, tile_gate(b, i * 2 + j) - 1)
                        split_main(b, i * 2 + (SLOT_GA + j), i + SLOT_GA // 2, j)
                with pool.Fori(0, 4) as i:
                    split_pair(b, SLOT_A, i)
                with pool.Fori(0, 4) as g:
                    split_pair(b, SLOT_WIN, g, 4)
                    split_side(b, g + 8, 4, tile_window(b, g))
                    split_pair(b, SLOT_WIN + 2, g, 4)
                with pool.Fori(0, (NSLOT - SLOT_B) // 2) as i:
                    split_pair(b, SLOT_B, i)
                if not last:
                    split_main(b, NSLOT, NSLOT // 2, 0)

            pool.wait_ge(setup, 1)
            split_main(0, 0, 0, 0)
            with pool.Fori(0, NB - 1) as b:
                block_split(b, False)
            block_split(NB - 1, True)

        @block.tensor
        def _(pe):
            def product(g, k_tiles, width, first=True, last=True, begin=None):
                for i, (wh, wl, xh, xl) in enumerate(k_tiles):
                    for q, (w, x) in enumerate(((wh, xh), (wh, xl), (wl, xh))):
                        for c in range(CH):
                            mm = nc.tensor.matmul(ps[:, g, c, 0:width], w, x[:, c * width:(c + 1) * width],
                                                  start=(first and i == 0 and q == 0),
                                                  stop=(last and i == len(k_tiles) - 1 and q == 2))
                            if begin is not None and i == q == c == 0:
                                mm.then_inc(begin, 1)
                return mm

            def full(b, pos, par, g, use, xh, xl, before=(), order=range(KT)):
                pe.wait_ge(main_split, b * NSLOT + pos + 3)
                pe.wait_ge(drained[g], use + 1)
                for i, k in enumerate(order):
                    for s, v in dict(before).get(i, ()):
                        pe.wait_ge(s, v)
                    mm = product(g, [(whi[:, par, k], wlo[:, par, k], xh[:, k, :], xl[:, k, :])], CW,
                                 i == 0, i == KT - 1, main_begun if i == 0 else None)
                mm.then_inc(ready, 1)

            def norm_sum(q, use):
                pe.wait_ge(drained[3], use + 1)
                for c in range(CH):
                    mm = nc.tensor.matmul(ps[:, 3, c, 0:CW], ones[:], tmp[:, q, c * CW:(c + 1) * CW], start=True, stop=True)
                mm.then_inc(ready, 1)

            def first_xa(b, ahead):
                full(b, 0, 0, 0, b * USE[0], xhi, xlo, order=XORDER,
                     before={i: ((xg_hi, b * 8 + i + 1), (xg_lo, b * 8 + i + 1)) for i in range(KT)})
                pe.wait_ge(q1_sum, b * 8 + 8)
                norm_sum(7, b * USE[3] + ahead)

            def block_products(b, last):
                n8 = b * 8
                full(b, 1, 1, 1, b * USE[1], xhi, xlo)
                with pe.Fori(0, 3) as i:
                    for j in range(2):
                        full(b, i * 2 + (2 + j), j, j, b * USE[0] + i + 1, xhi, xlo)
                with pe.Fori(0, 4) as i:
                    for j in range(2):
                        h = i * 2 + j
                        pe.wait_ge(side_split, b * 12 + h + 2)
                        pe.wait_ge(c_hi, n8 + h + 1)
                        pe.wait_ge(c_lo, n8 + h + 1)
                        for q in range(2):
                            pe.wait_ge(drained[2 + q], gate_use(b, q, h) + 1)
                            pe.nop(nofuse=True)
                            product(2 + q, [(shi[:, q], slo[:, q], yhi[:, h, :], ylo[:, h, :])], TC // CH).then_inc(ready, 1)
                        full(b, i * 2 + (SLOT_GA + j), j, j, b * USE[j] + i + 4, xhi, xlo)
                with pe.Fori(0, 4) as i:
                    for j in range(2):
                        full(b, i * 2 + (SLOT_A + j), j, j, b * USE[j] + i + 8, yhi, ylo,
                             before={0: ((ya_hi, n8 * 2 + 14), (ya_lo, n8 * 2 + 14)),
                                     KT - 1: ((ya_hi, n8 * 2 + 16), (ya_lo, n8 * 2 + 16))} if j == 0 else ())
                with pe.Fori(0, 4) as g:
                    full(b, g * 4 + SLOT_WIN, 0, 0, b * USE[0] + g * 2 + 12, xhi, xlo)
                    full(b, g * 4 + (SLOT_WIN + 1), 1, 1, b * USE[1] + g * 2 + 12, xhi, xlo)
                    full(b, g * 4 + (SLOT_WIN + 2), 0, 2, b * USE[2] + g + 8, xhi, xlo)
                    full(b, g * 4 + (SLOT_WIN + 3), 1, 3, b * USE[3] + g + 9, xhi, xlo)
                    pe.wait_ge(side_split, b * 12 + g + 10)
                    pe.wait_ge(d_hi, n8 * 2 + g * 4 + 4)
                    pe.wait_ge(d_lo, n8 * 2 + g * 4 + 4)
                    for m in range(2):
                        pe.wait_ge(drained[m], b * USE[m] + g * 2 + 14)
                        pe.nop(nofuse=True)
                        product(m, [(shi[:, 2 * m + k], slo[:, 2 * m + k], yhi[:, g * 2 + k, :], ylo[:, g * 2 + k, :])
                                    for k in range(2)], CW).then_inc(ready, 1)
                with pe.Fori(0, 4) as i:
                    for j in range(2):
                        full(b, i * 2 + (SLOT_B + j), j, j, b * USE[j] + i + 20, yhi, ylo,
                             before={KT - 1: ((drained[1], b * USE[1] + 21),)} if j == 0 else ())
                with pe.Fori(0, 4) as i:
                    for j in range(2):
                        full(b, i * 2 + (SLOT_O + j), j, j, b * USE[j] + i + 24, xhi, xlo,
                             before={0: ((m_hi, n8 + 7), (m_lo, n8 + 7)),
                                     KT - 1: ((m_hi, n8 + 8), (m_lo, n8 + 8))} if j == 0 else ())
                pe.wait_ge(q2_sum, n8 + 8)
                norm_sum(6, b * USE[3] + 13)
                with pe.Fori(0, PAIRS) as i:
                    for j in range(2):
                        full(b, i * 6 + (SLOT_MLP + 2 * j), 0, 2 * j, mlp_use(b, 2 * j, i), yhi, ylo,
                             before={0: ((x1_hi, n8 + 8), (x1_lo, n8 + 8))} if j == 0 else ())
                        full(b, i * 6 + (SLOT_MLP + 2 * j + 1), 1, 2 * j + 1, mlp_use(b, 2 * j + 1, i), yhi, ylo)
                    h = b * FT + i * 2
                    order = [(0, 0), (1, 0), (2, 0), (0, 1), (1, 1), (2, 1)] + [(m, k) for m in range(3, 8) for k in range(2)]
                    for m, k in order:
                        par = m // 4
                        if k == 0:
                            if m % 4 == 0:
                                pe.wait_ge(main_split, b * NSLOT + i * 6 + (SLOT_MLP + 4 + par + 3))
                            if m == 0:
                                pe.wait_ge(h_hi, h + 1)
                                pe.wait_ge(h_lo, h + 1)
                            pe.wait_ge(drained[m % 4], mlp_use(b, m % 4, i) + (2 + par))
                        if (m, k) == (0, 1):
                            pe.wait_ge(h_hi, h + 2)
                            pe.wait_ge(h_lo, h + 2)
                        w = 2 * (m % 4) + k
                        mm = product(m % 4, [(whi[:, par, w], wlo[:, par, w], xhi[:, k, :], xlo[:, k, :])], CW,
                                     k == 0, k == 1, main_begun if (m % 4, k) == (0, 0) else None)
                        if k == 1:
                            mm.then_inc(ready, 1)
                if not last:
                    first_xa(b + 1, -1)
                pe.wait_ge(q3_sum, n8 + 8)
                norm_sum(6, b * USE[3] + (47 if last else 48))

            pe.wait_ge(setup, 1)
            first_xa(0, 0)
            with pe.Fori(0, NB - 1) as b:
                block_products(b, False)
            block_products(NB - 1, True)

        @block.scalar
        def _(act):
            def load_x(b, k, j):
                act.dma_start(xin[:, j, :], dx[b, k]).then_inc(x_in[j], 16)

            def make_xg(b, pos, ahead=True):
                k, j, n = XORDER[pos], pos % 2, b * 8 + pos + 1
                act.wait_ge(x_in[j], (b * 8 + pos // 2 + 1) * 16)
                if pos == 6 and ahead:
                    act.wait_ge(ready, b * TILES - 1)
                nc.scalar.activation(xhi[:, k, :], xin[:, j, :], ACT.Copy, scale=cst[:, G1, bass.ds(k, 1)]).then_inc(xg_hi, 1)
                if pos >= 6 and ahead:
                    act.wait_ge(q3_sum, b * 8 + (pos - 7))
                nc.scalar.activation(tmp[:, 4 + j, 0:B], xin[:, j, :], ACT.Square).then_inc(x_sq, 1)
                act.wait_ge(q1_sum, n)
                act.wait_ge(x_sq, n)
                act.nop(nofuse=True)
                if pos < 6:
                    load_x(b, XORDER[pos + 2], j)
                else:
                    load_x(b, pos - 6, j)

            def root(r, tile):
                act.wait_ge(ready, tile + 1)
                nc.scalar.activation(two(rstd[:, r, :]), bank(3, 0, CW), ACT.Sqrt, bias=epsc[:, 0:1], scale=1.0 / D).then_inc(drained[3], 1)

            def conv(b, h, j, use):
                n = b * 8 + h + 1
                act.wait_ge(drained[j], use + 2)
                act.nop(nofuse=True)
                nc.scalar.activation(gate[:, h, :], tbuf[:, j, 3:3 + TC], ACT.Identity,
                                     bias=cst[:, CB, bass.ds(h, 1)], scale=cst[:, CW0 + 3, bass.ds(h, 1)]).then_inc(tap3, 1)
                act.wait_ge(tap, n * 3)
                act.nop(nofuse=True)
                nc.scalar.activation(yhi[:, h, :], gate[:, h, :], ACT.Copy).then_inc(c_hi, 1)

            def gates(b, h, j, prev=None):
                n, t = b * 8 + h + 1, tile_gate(b, h)
                tr, ti, ta, tq = (tmp[:, 4 * j + v, 0:TC] for v in range(4))
                if prev is not None:
                    sigmoid_a(b, *prev)
                act.wait_ge(ready, t + 1)
                act.nop(nofuse=True)
                nc.scalar.activation(two(tr), bank(2, 0, TC // 2), ACT.Sigmoid, bias=cst[:, BR, bass.ds(h, 1)]).then_inc(drained[2], 1)
                act.wait_ge(ready, t + 2)
                act.nop(nofuse=True)
                nc.scalar.activation(two(ti), bank(3, 0, TC // 2), ACT.Sigmoid, bias=cst[:, BI, bass.ds(h, 1)]).then_inc(drained[3], 1)
                act.wait_ge(drained[2], gate_use(b, 0, h) + 2)
                act.nop(nofuse=True)
                nc.scalar.activation(tq, tr, ACT.Tanh, scale=lac[:, 1, bass.ds(h, 1)]).then_inc(tanh_done, 1)
                nc.scalar.activation(ta, tr, ACT.Exp, scale=lac[:, 0, bass.ds(h, 1)]).then_inc(a_done, 1)
                if prev is not None:
                    out_hi(b, *prev)
                act.wait_ge(q_done, n)
                act.nop(nofuse=True)
                nc.scalar.activation(tq, tq, ACT.Sqrt).then_inc(mult_done, 1)

            def sigmoid_a(b, h, j, i):
                act.wait_ge(drained[j], b * USE[j] + i + 6)
                act.nop(nofuse=True)
                nc.scalar.activation(gate[:, h, 0:B], gate[:, h, 0:B], ACT.Sigmoid).then_inc(sig_a, 1)

            def out_hi(b, h, j, i):
                tr = tmp[:, 4 * j, :]
                act.wait_ge(scan_s, b * 8 + h + 1)
                act.nop(nofuse=True)
                nc.scalar.activation(prompt(yhi[:, h, 0:B]), two(tr[:, 0:PTOK]), ACT.Copy).then_inc(ya_hi, 1)
                nc.scalar.activation(sample(yhi[:, h, 0:B]), two(tr[:, PTOK + 3:PTOK + 3 + SCOL]), ACT.Copy).then_inc(ya_hi, 1)

            def square_x2(b, m):
                n = b * 8 + m + 1
                act.wait_ge(drained[m % 4], mlp_use(b, m % 4, PAIRS - 1) + (3 + m // 4))
                nc.scalar.activation(tmp[:, 4 + m % 2, 0:B], main[:, m, :], ACT.Square).then_inc(x2_sq, 1)

            def hidden(b, i, j):
                f = b * FT + i * 2 + (j + 1)
                act.wait_ge(drained[2 * j], mlp_use(b, 2 * j, i) + 2)
                nc.scalar.activation(tmp[:, j, 0:B], tmp[:, j, 0:B], ACT.Silu).then_inc(silu, 1)
                act.wait_ge(drained[2 * j + 1], mlp_use(b, 2 * j + 1, i) + 2)
                nc.scalar.activation(xhi[:, j, :], tmp[:, 2 + j, 0:B], ACT.Copy).then_inc(h_hi, 1)

            def block_act(b, last):
                n8 = b * 8
                conv(b, 1, 1, b * USE[1])
                with act.Fori(0, 3) as i:
                    for j in range(2):
                        conv(b, i * 2 + (2 + j), j, b * USE[j] + i + 1)
                gates(b, 0, 0)
                with act.Fori(0, 3) as i:
                    gates(b, i * 2 + 1, 1, (i * 2, 0, i))
                    gates(b, i * 2 + 2, 0, (i * 2 + 1, 1, i))
                gates(b, 7, 1, (6, 0, 3))
                out_hi(b, 7, 1, 3)
                sigmoid_a(b, 7, 1, 3)
                for g in range(4):
                    for j in range(2):
                        k, d = 2 * g + j, tmp[:, 4 * j + 2, :]
                        act.wait_ge(d_done, n8 + k + 1)
                        nc.scalar.activation(prompt(yhi[:, k, 0:B]), two(d[:, PH:PH + PTOK]), ACT.Copy).then_inc(d_hi, 1)
                        nc.scalar.activation(sample(yhi[:, k, 0:B]), two(d[:, 2 * PH + PTOK:TP]), ACT.Copy).then_inc(d_hi, 1)
                    for j in range(2):
                        k = 2 * g + j
                        act.wait_ge(drained[2 + j], b * USE[2 + j] + g + 10 + j)
                        nc.scalar.activation(gate[:, k, 0:B], gate[:, k, 0:B], ACT.Sigmoid).then_inc(sig_b, 1)
                    act.wait_ge(ready, tile_window(b, g) + 6)
                    for j in range(2):
                        k = 2 * g + j
                        nc.scalar.activation(two(yhi[:, k, 0:B]), bank(j, 0, CW), ACT.Copy, scale=cst[:, PSC, bass.ds(k, 1)]).then_inc(yb_hi, 1)
                with act.Fori(0, 4) as i:
                    for j in range(2):
                        m = i * 2 + j
                        act.wait_ge(merged, n8 + m + 1)
                        act.nop(nofuse=True)
                        nc.scalar.activation(xhi[:, m, :], main[:, m, :], ACT.Copy).then_inc(m_hi, 1)

                def residual(m, i, j):
                    act.wait_ge(drained[j], b * USE[j] + i + 26)
                    act.nop(nofuse=True)
                    nc.scalar.activation(yhi[:, m, 0:B], main[:, m, :], ACT.Copy, scale=cst[:, G2, bass.ds(m, 1)]).then_inc(x1_hi, 1)
                    nc.scalar.activation(tmp[:, 4 + j, 0:B], main[:, m, :], ACT.Square).then_inc(x1_sq, 1)

                with act.Fori(0, 3) as i:
                    for j in range(2):
                        residual(i * 2 + j, i, j)
                        load_x(b, i * 2 + (2 + j), j)
                for j in range(2):
                    residual(6 + j, 3, j)
                    if not last:
                        load_x(b + 1, XORDER[j], j)
                root(1, tile_norm2(b))
                with act.Fori(0, PAIRS - 1) as i:
                    hidden(b, i, 0)
                    hidden(b, i, 1)
                if not last:
                    for pos in range(6):
                        make_xg(b + 1, pos)
                hidden(b, PAIRS - 1, 0)
                hidden(b, PAIRS - 1, 1)
                for m in range(KT):
                    square_x2(b, m)
                if not last:
                    make_xg(b + 1, 6)
                    make_xg(b + 1, 7)
                    root(0, tile_norm2(b) + 134)
                    conv(b + 1, 0, 0, (b + 1) * USE[0])
                root(1, tile_norm2(b) + (133 if last else 135))
                for m in range(KT):
                    act.wait_ge(y_done, n8 + m + 1)
                    act.nop(nofuse=True)
                    act.dma_start(dy[b, m], main[:, m, :]).then_inc(y_stored, 16)

            act.wait_ge(setup, 1)
            act.wait_ge(lam_exp, 1)
            nc.scalar.activation(lac[:, 3, :], lac[:, 2, :], ACT.Exp, scale=-1.0).then_inc(lam_exp, 1)
            load_x(0, XORDER[0], 0)
            load_x(0, XORDER[1], 1)
            for pos in range(KT):
                make_xg(0, pos, False)
            act.wait_ge(lam_done, 1)
            root(0, 1)
            conv(0, 0, 0, 0)
            with act.Fori(0, NB - 1) as b:
                block_act(b, False)
            block_act(NB - 1, True)

        @block.vector
        def _(dve):
            V = nc.vector

            def make_xg(b, pos):
                k, j, n = XORDER[pos], pos % 2, b * 8 + pos + 1
                dve.wait_ge(x_in[j], (b * 8 + pos // 2 + 1) * 16)
                dve.wait_ge(xg_hi, n)
                V.scalar_tensor_tensor(xlo[:, k, :], xin[:, j, :], cst[:, G1, bass.ds(k, 1)], xhi[:, k, :].bitcast(f32), MUL, SUB).then_inc(xg_lo, 1)
                dve.wait_ge(x_sq, n)
                dve.wait_ge(q1_sum, n - 1) if pos else dve.wait_ge(q1_zero, b + 1)
                V.tensor_tensor(tmp[:, 7, 0:B], tmp[:, 7, 0:B], tmp[:, 4 + j, 0:B], ADD).then_inc(q1_sum, 1)

            def invert(r, use, done):
                dve.wait_ge(drained[3], use + 2)
                V.reciprocal(rstd[:, r, :], rstd[:, r, :]).then_inc(done, 1)

            def conv(b, h, j, use, tile):
                n, t = b * 8 + h + 1, tbuf[:, j, :]
                r2 = two(rstd[:, 0, :])
                V.tensor_copy(t[:, 0:3], state[:, h, S_CONV + 1:S_CONV + 4]).then_inc(xa_hist, 1)
                V.tensor_copy(t[:, PTOK + 3:PTOK + 6], state[:, h, S_CONV + 5:S_CONV + 8]).then_inc(xa_hist, 1)
                dve.wait_ge(ready, tile + 1)
                V.tensor_tensor(two(t[:, 3:3 + PTOK]), bank(j, 0, PC), r2[:, :, 0:PC], MUL).then_inc(xa_part, 1)
                V.tensor_tensor(two(t[:, PTOK + 6:PTOK + 6 + SCOL]), bank(j, PC, CW), r2[:, :, PC:CW], MUL).then_inc(drained[j], 1)
                dve.wait_ge(drained[j], use + 2)
                rows = t[:, PTOK - 1:PTOK - 1 + 28].rearrange("p (s n) -> p s n", s=2)[:, :, 0:4]
                V.tensor_copy(state[:, h, S_CONV:S_CONV + 8].rearrange("p (s n) -> p s n", s=2), rows).then_inc(xa_saved, 1)
                dve.wait_ge(tap3, n)
                for i, w in enumerate((2, 1, 0)):
                    if i:
                        dve.wait_ge(tap, (n - 1) * 3 + i)
                    V.scalar_tensor_tensor(gate[:, h, :], t[:, w:w + TC], cst[:, CW0 + w, bass.ds(h, 1)], gate[:, h, :], MUL, ADD).then_inc(tap, 1)
                dve.wait_ge(c_hi, n)
                V.tensor_tensor(ylo[:, h, :], gate[:, h, :], yhi[:, h, :].bitcast(f32), SUB).then_inc(c_lo, 1)

            def gates(b, h, j):
                n = b * 8 + h + 1
                tr, ti, ta, tq = (tmp[:, 4 * j + v, 0:TC] for v in range(4))
                dve.wait_ge(drained[3], gate_use(b, 1, h) + 2)
                V.tensor_tensor(ti, ti, gate[:, h, :], MUL).then_inc(ix_done, 1)
                dve.wait_ge(a_done, n)
                V.tensor_tensor(tr, ta, ta, MUL).then_inc(a2_done, 1)
                dve.wait_ge(a2_done, n)
                V.scalar_tensor_tensor(tq, tr, 1.0, tq, ADD, MUL).then_inc(q_done, 1)

            def recur(b, h, j):
                n = b * 8 + h + 1
                tr, ti, ta, tq = (tmp[:, 4 * j + v, :] for v in range(4))
                dve.wait_ge(mult_done, n)
                V.tensor_scalar(tq[:, 0:1], tq[:, 0:1], fix[:, 64:65], fix[:, 65:66], MUL, ADD).then_inc(pos0, 1)
                dve.wait_ge(pos0, n)
                V.tensor_tensor(ti[:, 0:TC], tq[:, 0:TC], ti[:, 0:TC], MUL).then_inc(bt_done, 1)
                dve.wait_ge(bt_done, n)
                s = PTOK + 3
                V.tensor_tensor_scan(tr[:, 0:PTOK], ta[:, 0:PTOK], ti[:, 0:PTOK], state[:, h, S_LRU + 1:S_LRU + 2], MUL, ADD).then_inc(scan_p, 1)
                V.tensor_tensor_scan(tr[:, s:s + SCOL], ta[:, s:s + SCOL], ti[:, s:s + SCOL], state[:, h, S_LRU + 3:S_LRU + 4], MUL, ADD).then_inc(scan_s, 1)
                dve.wait_ge(scan_s, n)
                last2 = tr[:, PTOK - 2:PTOK - 2 + 28].rearrange("p (s n) -> p s n", s=2)[:, :, 0:2]
                V.tensor_copy(state[:, h, S_LRU:S_LRU + 4].rearrange("p (s n) -> p s n", s=2), last2).then_inc(h_saved, 1)

            def gate_a(b, h, j, i):
                dve.wait_ge(ready, tile_gate(b, h) + 3)
                V.tensor_tensor(two(gate[:, h, 0:B]), bank(j, 0, CW), two(rstd[:, 0, :]), MUL).then_inc(drained[j], 1)

            def out_lo(b, h, j):
                tr = tmp[:, 4 * j, :]
                dve.wait_ge(ya_hi, (b * 8 + h + 1) * 2)
                V.tensor_tensor(prompt(ylo[:, h, 0:B]), two(tr[:, 0:PTOK]), prompt(yhi[:, h, 0:B]).bitcast(f32), SUB).then_inc(ya_lo, 1)
                V.tensor_tensor(sample(ylo[:, h, 0:B]), two(tr[:, PTOK + 3:PTOK + 3 + SCOL]), sample(yhi[:, h, 0:B]).bitcast(f32), SUB).then_inc(ya_lo, 1)

            def window(b, g, j):
                k = 2 * g + j
                n, t, w = b * 8 + k + 1, tbuf[:, j, :], WINDOWS[g]
                r2 = two(rstd[:, 0, :])
                V.tensor_copy(t[:, 0:PH], state[:, k, S_POOL + 1:S_POOL + 16]).then_inc(xb_hist, 1)
                V.tensor_copy(t[:, PTOK + PH:PTOK + 2 * PH], state[:, k, S_POOL + 17:S_POOL + 32]).then_inc(xb_hist, 1)
                dve.wait_ge(ready, tile_window(b, g) + (1 + j))
                V.tensor_tensor(two(t[:, PH:PH + PTOK]), bank(j, 0, PC), r2[:, :, 0:PC], MUL).then_inc(xb_part, 1)
                V.tensor_tensor(two(t[:, 2 * PH + PTOK:TP]), bank(j, PC, CW), r2[:, :, PC:CW], MUL).then_inc(drained[j], 1)
                dve.wait_ge(drained[j], b * USE[j] + 2 * g + 14)
                V.tensor_copy(state[:, k, S_POOL:S_POOL + 16], t[:, PTOK - 1:PTOK + 15]).then_inc(xb_saved, 1)
                V.tensor_copy(state[:, k, S_POOL + 16:S_POOL + 32], t[:, PTOK + 25:PTOK + 41]).then_inc(xb_saved, 1)
                src, span = t, 1
                steps = g + 1
                for q in range(steps):
                    out = tmp[:, 4 * j + q % 2, :]
                    if q:
                        dve.wait_ge(wsum, wsums(b, g, j) + q)
                    first = 2 * span - 1
                    V.tensor_tensor(out[:, first:TP], src[:, first:TP], src[:, first - span:TP - span], ADD).then_inc(wsum, 1)
                    src, span = out, 2 * span
                dve.wait_ge(wsum, wsums(b, g, j) + steps)
                V.tensor_tensor(src[:, PH:2 * PH], src[:, PH:2 * PH], fix[:, 16 * g:16 * g + PH], MUL).then_inc(wfix, 1)
                dve.wait_ge(wfix, n)
                d = tmp[:, 4 * j + 2, :]
                V.scalar_tensor_tensor(d[:, PH:TP], src[:, PH:TP], 1.0 / w, t[:, PH:TP], MUL, SUB).then_inc(d_done, 1)
                dve.wait_ge(d_hi, n * 2)
                V.tensor_tensor(prompt(ylo[:, k, 0:B]), two(d[:, PH:PH + PTOK]), prompt(yhi[:, k, 0:B]).bitcast(f32), SUB).then_inc(d_lo, 1)
                V.tensor_tensor(sample(ylo[:, k, 0:B]), two(d[:, 2 * PH + PTOK:TP]), sample(yhi[:, k, 0:B]).bitcast(f32), SUB).then_inc(d_lo, 1)

            def hidden(b, i, j):
                f, r2 = b * FT + i * 2 + (j + 1), two(rstd[:, 1, :])
                t, h = tmp[:, j, 0:B], tmp[:, 2 + j, 0:B]
                dve.wait_ge(ready, tile_mlp(b, i) + (1 + 2 * j))
                V.tensor_tensor(two(t), bank(2 * j, 0, CW), r2, MUL).then_inc(drained[2 * j], 1)
                dve.wait_ge(silu, f)
                V.tensor_tensor(t, t, rstd[:, 1, :], MUL).then_inc(sr_done, 1)
                dve.wait_ge(ready, tile_mlp(b, i) + (2 + 2 * j))
                dve.wait_ge(sr_done, f)
                V.tensor_tensor(two(h), bank(2 * j + 1, 0, CW), two(t), MUL).then_inc(drained[2 * j + 1], 1)
                dve.wait_ge(h_hi, f)
                V.tensor_tensor(xlo[:, j, :], h, xhi[:, j, :].bitcast(f32), SUB).then_inc(h_lo, 1)

            def add_down(b, i, m):
                dve.wait_ge(ready, tile_mlp(b, i) + (5 + m))
                V.tensor_tensor(two(main[:, m, :]), bank(m % 4, 0, CW), two(main[:, m, :]), ADD).then_inc(drained[m % 4], 1)

            def square_sum(b, m):
                n = b * 8 + m + 1
                dve.wait_ge(x2_sq, n)
                dve.wait_ge(q3_sum, n - 1) if m else dve.wait_ge(q3_zero, b + 1)
                V.tensor_tensor(tmp[:, 6, 0:B], tmp[:, 6, 0:B], tmp[:, 4 + m % 2, 0:B], ADD).then_inc(q3_sum, 1)

            def block_dve(b, last):
                n8 = b * 8
                conv(b, 1, 1, b * USE[1], tile_xa(b, 1))
                with dve.Fori(0, 3) as i:
                    for j in range(2):
                        conv(b, i * 2 + (2 + j), j, b * USE[j] + i + 1, tile_xa(b, i * 2 + (2 + j)))
                gates(b, 0, 0)
                with dve.Fori(0, 3) as i:
                    for j in range(2):
                        h = i * 2 + j
                        gate_a(b, h, j, i)
                        recur(b, h, j)
                        gates(b, h + 1, 1 - j)
                        out_lo(b, h, j)
                gate_a(b, 6, 0, 3)
                recur(b, 6, 0)
                gates(b, 7, 1)
                out_lo(b, 6, 0)
                recur(b, 7, 1)
                out_lo(b, 7, 1)
                gate_a(b, 7, 1, 3)
                dve.wait_ge(y_stored, b * (16 * KT) + 16)
                dve.nop(nofuse=True)
                with dve.Fori(0, 4) as i:
                    for j in range(2):
                        m = i * 2 + j
                        dve.wait_ge(sig_a, n8 + m + 1)
                        dve.wait_ge(ready, tile_a(b, m) + 1)
                        V.tensor_tensor(two(main[:, m, :]), bank(j, 0, CW), two(gate[:, m, 0:B]), MUL).then_inc(drained[j], 1)
                for g in range(4):
                    window(b, g, 0)
                    window(b, g, 1)
                    for j in range(2):
                        dve.wait_ge(ready, tile_window(b, g) + (3 + j))
                        V.tensor_tensor(two(gate[:, 2 * g + j, 0:B]), bank(2 + j, 0, CW), two(rstd[:, 0, :]), MUL).then_inc(drained[2 + j], 1)
                    for j in range(2):
                        k = 2 * g + j
                        dve.wait_ge(yb_hi, n8 + k + 1)
                        V.scalar_tensor_tensor(two(ylo[:, k, 0:B]), bank(j, 0, CW), cst[:, PSC, bass.ds(k, 1)],
                                               two(yhi[:, k, 0:B]).bitcast(f32), MUL, SUB).then_inc(drained[j], 1)
                with dve.Fori(0, 4) as i:
                    for j in range(2):
                        m = i * 2 + j
                        dve.wait_ge(sig_b, n8 + m + 1)
                        dve.wait_ge(ready, tile_b(b, m) + 1)
                        V.tensor_tensor(two(tmp[:, j, 0:B]), bank(j, 0, CW), two(gate[:, m, 0:B]), MUL).then_inc(drained[j], 1)
                        dve.wait_ge(drained[j], b * USE[j] + i + 22)
                        V.tensor_tensor(main[:, m, :], main[:, m, :], tmp[:, j, 0:B], ADD).then_inc(merged, 1)
                        dve.wait_ge(m_hi, n8 + m + 1)
                        V.tensor_tensor(xlo[:, m, :], main[:, m, :], xhi[:, m, :].bitcast(f32), SUB).then_inc(m_lo, 1)
                V.memset(tmp[:, 6, 0:B], 0.0).then_inc(q2_zero, 1)
                with dve.Fori(0, 4) as i:
                    for j in range(2):
                        m = i * 2 + j
                        dve.wait_ge(x_in[j], (n8 + i + 5) * 16)
                        dve.wait_ge(ready, tile_o(b, m) + 1)
                        V.tensor_tensor(two(main[:, m, :]), bank(j, 0, CW), two(xin[:, j, :]), ADD).then_inc(drained[j], 1)
                        dve.wait_ge(x1_hi, n8 + m + 1)
                        V.scalar_tensor_tensor(ylo[:, m, 0:B], main[:, m, :], cst[:, G2, bass.ds(m, 1)], yhi[:, m, 0:B].bitcast(f32), MUL, SUB).then_inc(x1_lo, 1)
                        dve.wait_ge(x1_sq, n8 + m + 1)
                        V.tensor_tensor(tmp[:, 6, 0:B], tmp[:, 6, 0:B], tmp[:, 4 + j, 0:B], ADD).then_inc(q2_sum, 1)
                invert(1, b * USE[3] + 13, rstd2)
                dve.wait_ge(rstd2, b + 1)
                dve.nop(nofuse=True)
                with dve.Fori(0, PAIRS - 1) as i:
                    hidden(b, i, 0)
                    hidden(b, i, 1)
                    for m in range(KT):
                        add_down(b, i, m)
                if not last:
                    V.memset(tmp[:, 7, 0:B], 0.0).then_inc(q1_zero, 1)
                    for pos in range(6):
                        make_xg(b + 1, pos)
                hidden(b, PAIRS - 1, 0)
                hidden(b, PAIRS - 1, 1)
                V.memset(tmp[:, 6, 0:B], 0.0).then_inc(q3_zero, 1)
                for m in range(KT):
                    add_down(b, PAIRS - 1, m)
                    if m:
                        square_sum(b, m - 1)
                square_sum(b, KT - 1)
                if not last:
                    V.memset(fix[:, 0:65], 1.0).then_inc(unfix, 1)
                    V.memset(fix[:, 65:66], 0.0).then_inc(unfix, 1)
                    make_xg(b + 1, 6)
                    make_xg(b + 1, 7)
                    invert(0, (b + 1) * USE[3] - 1, rstd1)
                    dve.wait_ge(rstd1, b + 2)
                    conv(b + 1, 0, 0, (b + 1) * USE[0], tile_xa(b + 1, -2))
                invert(1, b * USE[3] + (47 if last else 48), rstd3)
                dve.wait_ge(rstd3, b + 1)
                dve.nop(nofuse=True)
                with dve.Fori(0, KT) as m:
                    V.scalar_tensor_tensor(main[:, m, :], main[:, m, :], cst[:, GF, bass.ds(m, 1)], rstd[:, 1, :], MUL, MUL).then_inc(y_done, 1)

            V.memset(credit[:, 0:1], 0.0).then_inc(main_split, 2)
            V.memset(credit[:, 1:2], 0.0).then_inc(main_begun, 1)
            V.memset(credit[:, 2:3], 0.0).then_inc(side_split, 1)
            V.memset(credit[:, 3:4], 0.0).then_inc(y_stored, 16)
            for g in range(4):
                V.memset(credit[:, 4 + g:5 + g], 0.0).then_inc(drained[g], 1)
            V.memset(tmp[:, 7, 0:B], 0.0).then_inc(q1_zero, 1)
            V.memset(tbuf[:, :, 706:708], 0.0)
            V.memset(epsc[:], EPS)
            V.memset(ones[:], 1.0).then_inc(setup, 1)
            dve.wait_ge(consts_in, 48)
            chain = [0]

            def link(ins):
                chain[0] += 1
                ins.then_inc(lam_chain, 1)
                dve.wait_ge(lam_chain, chain[0])

            lam = cst[:, LAM, :]
            link(V.tensor_scalar(lac[:, 2, :], lam, -1.0, None, MUL))
            V.tensor_tensor(lac[:, 2, :], lac[:, 2, :], lam, ALU.max).then_inc(lam_exp, 1)
            dve.wait_ge(lam_exp, 2)
            link(V.tensor_scalar(lac[:, 4, :], lac[:, 3, :], 2.0, None, ADD))
            link(V.reciprocal(lac[:, 4, :], lac[:, 4, :]))
            link(V.tensor_tensor(lac[:, 3, :], lac[:, 3, :], lac[:, 4, :], MUL))
            link(V.tensor_tensor(lac[:, 4, :], lac[:, 3, :], lac[:, 3, :], MUL))
            link(V.tensor_scalar(lac[:, 5, :], lac[:, 4, :], 1.0 / 17, None, MUL))
            for q in (15, 13, 11, 9, 7, 5, 3):
                link(V.scalar_tensor_tensor(lac[:, 5, :], lac[:, 5, :], 1.0 / q, lac[:, 4, :], ADD, MUL))
            link(V.scalar_tensor_tensor(lac[:, 5, :], lac[:, 5, :], 1.0, lac[:, 3, :], ADD, MUL))
            link(V.tensor_scalar(lac[:, 6, :], lam, 0.0, None, ALU.min))
            link(V.scalar_tensor_tensor(lac[:, 5, :], lac[:, 5, :], -2.0, lac[:, 6, :], MUL, ADD))
            link(V.tensor_scalar(lac[:, 0, :], lac[:, 5, :], LRU_C, None, MUL))
            V.tensor_scalar(lac[:, 1, :], lac[:, 5, :], -LRU_C, None, MUL).then_inc(lam_done, 1)
            for pos in range(KT):
                make_xg(0, pos)
            invert(0, 0, rstd1)
            dve.wait_ge(rstd1, 1)
            conv(0, 0, 0, 0, 0)
            with dve.Fori(0, NB - 1) as b:
                block_dve(b, False)
            block_dve(NB - 1, True)


def kernel(x_prompt, x_sample, state_conv, state_lru, state_pool, meta_tokens, norm1_g, w_in, conv_w, conv_b,
           lam, w_r, b_r, w_i, b_i, pool_w, pool_scale, w_br_a, w_br_b, w_out, norm2_g, w_gu, w_down, final_g):
    import concourse.bacc as _bacc
    from concourse.bass_utils import run_bass_kernel_spmd as _run

    A = np.asarray
    prompt = np.concatenate([A(meta_tokens), A(x_prompt)[0]], axis=0).reshape(NB, CH, PC, D)
    sample = np.concatenate([A(x_sample)[0], np.zeros((NB * STOK - DEC, D), np.float32)], axis=0).reshape(NB, STOK, D)
    sample = np.concatenate([sample, np.zeros((NB, 1, D), np.float32)], axis=1).reshape(NB, CH, SC, D)
    dx = np.concatenate([prompt, sample], axis=2).reshape(NB, B, KT, P).transpose(0, 2, 3, 1)

    def columns(w, c0, n):
        w = A(w)[:, c0:c0 + n * P]
        return w.reshape(KT, P, n, P).transpose(2, 1, 0, 3).reshape(n, P, KT * P)

    w_in, w_gu = A(w_in)[0], A(w_gu)[0]
    xb, gb = columns(w_in, D, KT), columns(w_in, 3 * D, KT)
    hg, hu = columns(w_gu, 0, FT), columns(w_gu, FF, FT)
    down = A(w_down)[0].reshape(PAIRS, 2, P, 2, 4, P).transpose(0, 3, 2, 4, 1, 5).reshape(PAIRS, 2, P, KT * P)
    slots = [columns(w_in, 0, KT), columns(w_in, 2 * D, KT), columns(A(w_br_a)[0], 0, KT)]
    for g in range(4):
        slots += [xb[2 * g:2 * g + 2], gb[2 * g:2 * g + 2]]
    slots += [columns(A(w_br_b)[0], 0, KT), columns(A(w_out)[0], 0, KT)]
    for i in range(PAIRS):
        slots += [hg[2 * i:2 * i + 1], hu[2 * i:2 * i + 1], hg[2 * i + 1:2 * i + 2], hu[2 * i + 1:2 * i + 2], down[i]]
    dwm = np.concatenate(slots, axis=0)
    ri = np.concatenate([A(w_r)[0], A(w_i)[0], np.zeros((KT, P, 2 * P), np.float32)], axis=2)
    pw = A(pool_w)[0].reshape(4, 2, P, 2, P).transpose(0, 2, 3, 1, 4).reshape(4, P, 4 * P)
    dws = np.concatenate([ri, pw], axis=0)
    rows = [A(norm1_g), A(conv_w)[0], A(conv_b), A(b_r), A(b_i), A(lam), A(pool_scale), A(norm2_g), A(final_g)[None]]
    dcst = np.concatenate(rows, axis=0).reshape(NCST, KT, P).transpose(2, 0, 1)
    fix = np.ones((P, 66), np.float32)
    for g, w in enumerate(WINDOWS):
        for t in range(w - 1):
            fix[:, 16 * g + t] = w / (t + 1)
    fix[:, 64] = 0.0
    st0 = np.zeros((P, KT, NST), np.float32)
    st0[:, :, S_CONV + 5:S_CONV + 8] = A(state_conv)[0, 0].reshape(3, KT, P).transpose(2, 1, 0)
    st0[:, :, S_LRU + 3] = A(state_lru)[0, 0].reshape(KT, P).transpose(1, 0)
    st0[:, :, S_POOL + 17:S_POOL + 32] = A(state_pool)[0, 0].reshape(PH, KT, P).transpose(2, 1, 0)

    nc = _bacc.Bacc("TRN2", target_bir_lowering=False, num_devices=1)
    arrays = {"dx": dx, "dwm": dwm, "dws": dws, "dcst": dcst, "dfix": fix, "dst0": st0}
    arrays = {k: np.ascontiguousarray(v) for k, v in arrays.items()}
    ins = [nc.dram_tensor(k, v.shape, mybir.dt.float32, kind="ExternalInput").ap() for k, v in arrays.items()]
    dy = nc.dram_tensor("dy", (NB, KT, P, B), mybir.dt.float32, kind="ExternalOutput").ap()
    dst = nc.dram_tensor("dst", (P, KT, NST), mybir.dt.float32, kind="ExternalOutput").ap()
    build(nc, *ins, dy, dst)
    r = _run(nc, [arrays], core_ids=[0]).results[0]

    y = A(r["dy"]).transpose(0, 3, 1, 2).reshape(NB, CH, CW, D)
    yp = y[:, :, 0:PC].reshape(1, SEQ + META, D)[:, META:]
    ys = y[:, :, PC:CW].reshape(NB, SCOL, D)[:, 0:STOK].reshape(1, NB * STOK, D)[:, 0:DEC]
    st = A(r["dst"]).transpose(2, 1, 0).reshape(NST, D)

    def rows_of(first, n):
        return np.ascontiguousarray(st[first:first + n])[None, None]

    return (np.ascontiguousarray(yp), np.ascontiguousarray(ys),
            rows_of(S_CONV + 1, 3), rows_of(S_LRU + 1, 1)[:, :, 0], rows_of(S_POOL + 1, PH),
            rows_of(S_CONV + 4, 3), rows_of(S_LRU + 2, 1)[:, :, 0], rows_of(S_POOL + 16, PH))
```

```python
import numpy as np
import concourse.bass as bass
from concourse import mybir
from contextlib import ExitStack

P = 128
D = 1024
KT = D // P
SEQ, META, DEC, PAST = 2048, 16, 32, 512
NB = 3
CH = 2
PTOK = (SEQ + META) // NB
STOK = -(-DEC // NB)
SCOL = STOK + 1
PC, SC = PTOK // CH, SCOL // CH
CW = PC + SC
B = CH * CW
CONV = 4
TC = PTOK + (CONV - 1) + SCOL + 1
WINDOWS = (2, 4, 8, 16)
PH = 15
TP = PH + PTOK + PH + SCOL
TW = 732
FF = 2816
FT = FF // P
PAIRS = FT // 2
EPS = 1e-6
LRU_C = 8.0
G1, CW0, CB, BR, BI, LAM, PSC, G2, GF = 0, 1, 5, 6, 7, 8, 9, 10, 11
NCST = 12
YV = 5
S_CONV, S_LRU, S_POOL, NST = 0, 8, 12, 44
XORDER = [2, 3, 4, 5, 6, 7, 0, 1]
SLOT_XA, SLOT_GA, SLOT_XB, SLOT_A, SLOT_WIN, SLOT_B, SLOT_O, SLOT_MLP = 0, 8, 16, 18, 26, 40, 48, 56
NSLOT = SLOT_MLP + 6 * PAIRS
USE = (57, 57, 49, 52)
TILES = 215


def tile_xa(b, h):
    return b * TILES + h + 1


def tile_ga(b, h):
    return b * TILES + h * 3 + 9


def tile_xb(b, g, j):
    return b * TILES + (33 if g == 0 else 39 + 6 * g) + j


def tile_a(b, m):
    return b * TILES + m + 35


def tile_gb(b, g, j):
    return b * TILES + g * 6 + (43 + j)


def tile_win(b, g, m):
    return b * TILES + (47 + 6 * g if g < 3 else 63) + m


def tile_b(b, m):
    return b * TILES + m + 65


def tile_o(b, m):
    return b * TILES + m + 73


def tile_mlp(b, i):
    return b * TILES + i * 12 + 82


def tile_norm(b, which, last=False):
    return b * TILES + (82, 215, 214 if last else 216)[which]


def gate_use(b, q, h):
    return b * USE[2 + q] + h + q


def xb_use(b, g):
    return b * USE[0] + (8 if g == 0 else 11 + 2 * g)


def win_use(b, g):
    return b * USE[0] + (14 + 2 * g if g < 3 else 19)


def mlp_use(b, g, i):
    return b * USE[g] + i * 3 + (24, 24, 16, 18)[g]


def wsums(b, g, j):
    return b * 20 + 2 * (g * (g + 1) // 2) + j * (g + 1)


def build(nc, dx, dwm, dws, dcst, dfix, dst0, dy, dst):
    f32 = mybir.dt.float32
    f32r = mybir.dt.float32r
    ALU = mybir.AluOpType
    ACT = mybir.ActivationFunctionType
    MUL, ADD, SUB = ALU.mult, ALU.add, ALU.subtract
    ctx = ExitStack()
    with ctx:
        def sb(name, shape, dt=f32):
            return ctx.enter_context(nc.sbuf_tensor(name, shape, dt))

        def sem(name):
            return ctx.enter_context(nc.semaphore(name))

        xhi, xlo = sb("xhi", [P, KT, B], f32r), sb("xlo", [P, KT, B], f32r)
        yhi, ylo = sb("yhi", [P, KT, TC], f32r), sb("ylo", [P, KT, TC], f32r)
        main = sb("main", [P, KT, B])
        gate = sb("gate", [P, KT, TC])
        wraw = sb("wraw", [P, 2, KT * P])
        whi, wlo = sb("whi", [P, 2, KT, P], f32r), sb("wlo", [P, 2, KT, P], f32r)
        sraw = sb("sraw", [P, 4 * P])
        shi, slo = sb("shi", [P, 4, P], f32r), sb("slo", [P, 4, P], f32r)
        rstd = sb("rstd", [P, 2, B])
        tmp = sb("tmp", [P, 8, TW])
        tbuf = sb("tbuf", [P, 2, TW])
        xin = sb("xin", [P, 2, B])
        state = sb("state", [P, KT, NST])
        cst = sb("cst", [P, NCST, KT])
        lac = sb("lac", [P, 8, KT])
        fix = sb("fix", [P, 66])
        ones = sb("ones", [P, P])
        epsc = sb("epsc", [P, 1])
        credit = sb("credit", [P, 8])
        ps = ctx.enter_context(nc.psum_tensor("ps", [P, 4, CH, 512], f32))

        consts_in, tables_in = sem("consts_in"), sem("tables_in")
        x_in = [sem("x_in0"), sem("x_in1")]
        x0_in = [sem(f"x0_in{pos}") for pos in range(KT)]
        main_in = [sem("main_in0"), sem("main_in1")]
        side_in = sem("side_in")
        y_stored = sem("y_stored")
        state_stored = sem("state_stored")
        main_hi, main_split, main_begun = sem("main_hi"), sem("main_split"), sem("main_begun")
        side_hi, side_split = sem("side_hi"), sem("side_split")
        ready = sem("psum_ready")
        drained = [sem(f"psum_drained{g}") for g in range(4)]
        setup = sem("setup")
        lam_exp, lam_chain, lam_done = sem("lam_exp"), sem("lam_chain"), sem("lam_done")
        xg_hi, xg_lo, x_sq, q1_zero, q1_sum, rstd1 = (sem(n) for n in ("xg_hi", "xg_lo", "x_sq", "q1_zero", "q1_sum", "rstd1"))
        xa_hist, xa_part, xa_saved, tap3, tap, c_hi, c_lo = (sem(n) for n in ("xa_hist", "xa_part", "xa_saved", "tap3", "tap", "c_hi", "c_lo"))
        tanh_done, a_done, mult_done, ix_done, a2_done, q_done = (sem(n) for n in ("tanh_done", "a_done", "mult_done", "ix_done", "a2_done", "q_done"))
        pos0, bt_done, scan_p, scan_s, h_saved, ya_hi, ya_lo, sig_a = (sem(n) for n in ("pos0", "bt_done", "scan_p", "scan_s", "h_saved", "ya_hi", "ya_lo", "sig_a"))
        xb_hist, xb_part, xb_saved, wsum, wfix, d_done, d_hi, d_lo, yb_hi, sig_b = (sem(n) for n in (
            "xb_hist", "xb_part", "xb_saved", "wsum", "wfix", "d_done", "d_hi", "d_lo", "yb_hi", "sig_b"))
        merged, m_hi, m_lo = sem("merged"), sem("m_hi"), sem("m_lo")
        x1_hi, x1_lo, x1_sq, q2_zero, q2_sum, rstd2 = (sem(n) for n in ("x1_hi", "x1_lo", "x1_sq", "q2_zero", "q2_sum", "rstd2"))
        silu, sr_done, h_hi, h_lo = sem("silu"), sem("sr_done"), sem("h_hi"), sem("h_lo")
        x2_sq, q3_zero, q3_sum, rstd3, y_gain, y_done, y_last, unfix = (sem(n) for n in ("x2_sq", "q3_zero", "q3_sum", "rstd3", "y_gain", "y_done", "y_last", "unfix"))

        block = ctx.enter_context(nc.Block())

        def bank(g, c0, c1):
            return ps[:, g, :, c0:c1]

        def two(ap):
            return ap.rearrange("p (c n) -> p c n", c=CH)

        def prompt(t):
            return two(t)[:, :, 0:PC]

        def sample(t):
            return two(t)[:, :, PC:CW]

        @block.sync
        def _(sp):
            sp.dma_start(cst[:], dcst).then_inc(consts_in, 16)

            def load_main(b, pos, par):
                sp.wait_ge(main_split, b * NSLOT + pos + 1)
                sp.nop(nofuse=True)
                sp.dma_start(wraw[:, par, :], dwm[pos]).then_inc(main_in[par], 16)

            def load_side(b, s, width):
                sp.wait_ge(side_split, b * 12 + s + 1)
                sp.nop(nofuse=True)
                sp.dma_start(sraw[:, 0:width], dws[s, :, 0:width]).then_inc(side_in, 16)

            def block_loads(b, last):
                load_main(b, 1, 1)
                with sp.Fori(0, 3) as i:
                    load_main(b, SLOT_XA + 2 + i * 2, 0)
                    load_main(b, SLOT_XA + 3 + i * 2, 1)
                with sp.Fori(0, 4) as i:
                    for j in range(2):
                        load_main(b, SLOT_GA + j + i * 2, j)
                        load_side(b, i * 2 + j, 2 * P)
                with sp.Fori(0, (SLOT_WIN - SLOT_XB) // 2) as i:
                    for j in range(2):
                        load_main(b, SLOT_XB + j + i * 2, j)
                with sp.Fori(0, 3) as g:
                    load_main(b, SLOT_WIN + g * 4, 0)
                    load_main(b, SLOT_WIN + 1 + g * 4, 1)
                    load_side(b, g + 8, 4 * P)
                    load_main(b, SLOT_WIN + 2 + g * 4, 0)
                    load_main(b, SLOT_WIN + 3 + g * 4, 1)
                load_main(b, SLOT_B - 2, 0)
                load_main(b, SLOT_B - 1, 1)
                load_side(b, 11, 4 * P)
                with sp.Fori(0, (NSLOT - SLOT_B) // 2) as i:
                    for j in range(2):
                        load_main(b, SLOT_B + j + i * 2, j)
                if not last:
                    sp.wait_ge(main_split, (b + 1) * NSLOT + 1)
                    sp.nop(nofuse=True)
                    sp.dma_start(wraw[:, 0, :], dwm[0]).then_inc(main_in[0], 16)

            sp.wait_ge(setup, 1)
            load_main(0, 0, 0)
            for pos in (1, 3, 5, 7):
                sp.dma_start(main[:, XORDER[pos], :], dx[0, XORDER[pos]]).then_inc(x0_in[pos], 16)
            for dst_, src_ in ((fix, dfix), (state, dst0)):
                sp.dma_start(dst_[:], src_).then_inc(tables_in, 16)
            with sp.Fori(0, NB - 1) as b:
                block_loads(b, False)
            block_loads(NB - 1, True)
            sp.wait_ge(h_saved, 8 * NB)
            sp.wait_ge(xb_saved, 16 * NB)
            sp.dma_start(dst, state[:]).then_inc(state_stored, 16)
            for m in range(YV, KT):
                sp.wait_ge(y_done, 8 * (NB - 1) + m - YV + 1)
                sp.dma_start(dy[NB - 1, m], main[:, m, :]).then_inc(y_stored, 16)
            sp.wait_ge(state_stored, 16)
            sp.wait_ge(y_stored, 16 + 16 * KT * NB)

        @block.gpsimd
        def _(pool):
            def split_main(b, pos, half, par):
                n = b * NSLOT + pos
                pool.wait_ge(main_in[par], (b * (NSLOT // 2) + half + 1) * 16)
                pool.nop(nofuse=True)
                pool.wait_ge(main_begun, n + 1)
                pool.nop(nofuse=True)
                nc.gpsimd.tensor_scalar(whi[:, par].rearrange("p k c -> p (k c)"), wraw[:, par, :], 1.0, 1.0, MUL, MUL).then_inc(main_hi, 1)
                pool.wait_ge(main_hi, n + 1)
                pool.nop(nofuse=True)
                nc.gpsimd.tensor_tensor(wlo[:, par].rearrange("p k c -> p (k c)"), wraw[:, par, :],
                                        whi[:, par].rearrange("p k c -> p (k c)").bitcast(f32), SUB).then_inc(main_split, 1)

            def split_pair(b, first, i, step=2):
                for j in range(2):
                    split_main(b, i * step + (first + j), i * (step // 2) + first // 2, j)

            def split_side(b, s, tiles, free):
                n = b * 12 + s
                pool.wait_ge(side_in, (n + 1) * 16)
                pool.nop(nofuse=True)
                pool.wait_ge(ready, free)
                pool.nop(nofuse=True)
                w = tiles * P
                hi2, lo2 = shi[:, :, :].rearrange("p k c -> p (k c)"), slo[:, :, :].rearrange("p k c -> p (k c)")
                nc.gpsimd.tensor_scalar(hi2[:, 0:w], sraw[:, 0:w], 1.0, 1.0, MUL, MUL).then_inc(side_hi, 1)
                pool.wait_ge(side_hi, n + 1)
                pool.nop(nofuse=True)
                nc.gpsimd.tensor_tensor(lo2[:, 0:w], sraw[:, 0:w], hi2[:, 0:w].bitcast(f32), SUB).then_inc(side_split, 1)

            def gain(m):
                nc.gpsimd.tensor_tensor(main[:, m, :], main[:, m, :], cst[:, GF, bass.ds(m, 1)].to_broadcast([P, B]), MUL).then_inc(y_gain, 1)

            def final(m, n):
                gain(m)
                pool.wait_ge(y_gain, n)
                pool.nop(nofuse=True)
                nc.gpsimd.tensor_tensor(main[:, m, :], main[:, m, :], rstd[:, 1, :], MUL).then_inc(y_done, 1)

            def split_to_heads(b, finals):
                split_main(b, 1, 0, 1)
                with pool.Fori(0, 3) as i:
                    split_pair(b, SLOT_XA + 2, i)
                with pool.Fori(0, 4) as i:
                    for j in range(2):
                        split_main(b, i * 2 + (SLOT_GA + j), i + SLOT_GA // 2, j)
                        split_side(b, i * 2 + j, 2, tile_ga(b, i * 2 + j))
                        if finals:
                            pool.wait_ge(rstd3, b)
                            pool.nop(nofuse=True)
                            final(i * 2 + j, b * 8 + i * 2 + (j - 7))

            def split_rest(b, last):
                with pool.Fori(0, (SLOT_WIN - SLOT_XB) // 2) as i:
                    split_pair(b, SLOT_XB, i)
                with pool.Fori(0, 3) as g:
                    split_pair(b, SLOT_WIN, g, 4)
                    split_side(b, g + 8, 4, tile_gb(b, g, 0))
                    split_pair(b, SLOT_WIN + 2, g, 4)
                split_pair(b, SLOT_B - 2, 0)
                split_side(b, 11, 4, tile_gb(b, 3, 0))
                with pool.Fori(0, (NSLOT - SLOT_B) // 2) as i:
                    split_pair(b, SLOT_B, i)
                if not last:
                    split_main(b, NSLOT, NSLOT // 2, 0)

            pool.wait_ge(setup, 1)
            split_main(0, 0, 0, 0)
            split_to_heads(0, False)
            with pool.Fori(0, NB - 1) as b:
                split_rest(b, False)
                split_to_heads(b + 1, True)
            split_rest(NB - 1, True)
            pool.wait_ge(q3_sum, 8 * NB)
            for m in range(YV, KT):
                gain(m)
            pool.wait_ge(y_gain, 8 * (NB - 1) + KT - YV)
            pool.wait_ge(rstd3, NB)
            for m in range(YV, KT):
                nc.gpsimd.tensor_tensor(main[:, m, :], main[:, m, :], rstd[:, 1, :], MUL).then_inc(y_done, 1)

        @block.tensor
        def _(pe):
            def product(g, k_tiles, width, first=True, last=True, begin=None):
                for i, (wh, wl, xh, xl) in enumerate(k_tiles):
                    for q, (w, x) in enumerate(((wh, xh), (wh, xl), (wl, xh))):
                        for c in range(CH):
                            mm = nc.tensor.matmul(ps[:, g, c, 0:width], w, x[:, c * width:(c + 1) * width],
                                                  start=(first and i == 0 and q == 0),
                                                  stop=(last and i == len(k_tiles) - 1 and q == 2))
                            if begin is not None and i == q == c == 0:
                                mm.then_inc(begin, 1)
                return mm

            def full(b, pos, par, g, use, xh, xl, before=(), order=range(KT)):
                pe.wait_ge(main_split, b * NSLOT + pos + 3)
                pe.wait_ge(drained[g], use + 1)
                for i, k in enumerate(order):
                    for s, v in dict(before).get(i, ()):
                        pe.wait_ge(s, v)
                    mm = product(g, [(whi[:, par, k], wlo[:, par, k], xh[:, k, :], xl[:, k, :])], CW,
                                 i == 0, i == KT - 1, main_begun if i == 0 else None)
                mm.then_inc(ready, 1)

            def norm_sum(q, use):
                pe.wait_ge(drained[3], use + 1)
                for c in range(CH):
                    mm = nc.tensor.matmul(ps[:, 3, c, 0:CW], ones[:], tmp[:, q, c * CW:(c + 1) * CW], start=True, stop=True)
                mm.then_inc(ready, 1)

            def first_xa(b, ahead):
                full(b, 0, 0, 0, b * USE[0], xhi, xlo, order=XORDER,
                     before={i: ((xg_hi, b * 8 + i + 1), (xg_lo, b * 8 + i + 1)) for i in range(KT)})
                pe.wait_ge(q1_sum, b * 8 + 8)
                norm_sum(7, b * USE[3] + ahead)

            def block_products(b, last):
                n8 = b * 8
                full(b, 1, 1, 1, b * USE[1], xhi, xlo)
                with pe.Fori(0, 3) as i:
                    for j in range(2):
                        full(b, i * 2 + (2 + j), j, j, b * USE[0] + i + 1, xhi, xlo)
                with pe.Fori(0, 4) as i:
                    for j in range(2):
                        h = i * 2 + j
                        full(b, i * 2 + (SLOT_GA + j), j, j, b * USE[j] + i + 4, xhi, xlo)
                        pe.wait_ge(side_split, b * 12 + h + 2)
                        pe.wait_ge(c_hi, n8 + h + 1)
                        pe.wait_ge(c_lo, n8 + h + 1)
                        for q in range(2):
                            pe.wait_ge(drained[2 + q], gate_use(b, q, h) + 1)
                            pe.nop(nofuse=True)
                            product(2 + q, [(shi[:, q], slo[:, q], yhi[:, h, :], ylo[:, h, :])], TC // CH).then_inc(ready, 1)

                def xb_pair(g, i, use):
                    for j in range(2):
                        full(b, (SLOT_XB + j) if g == 0 else i * 4 + (SLOT_WIN + 2 + j), j, j, use, xhi, xlo)

                def gb_pair(g):
                    full(b, g * 4 + SLOT_WIN, 0, 2, b * USE[2] + g + 8, xhi, xlo)
                    full(b, g * 4 + (SLOT_WIN + 1), 1, 3, b * USE[3] + g + 9, xhi, xlo)

                def project(g, use):
                    pe.wait_ge(side_split, b * 12 + g + 10)
                    pe.wait_ge(d_hi, n8 * 2 + g * 4 + 4)
                    pe.wait_ge(d_lo, n8 * 2 + g * 4 + 4)
                    for m in range(2):
                        pe.wait_ge(drained[m], use + 1)
                        pe.nop(nofuse=True)
                        product(m, [(shi[:, 2 * m + k], slo[:, 2 * m + k], yhi[:, g * 2 + k, :], ylo[:, g * 2 + k, :])
                                    for k in range(2)], CW).then_inc(ready, 1)

                xb_pair(0, 0, xb_use(b, 0))
                with pe.Fori(0, 4) as i:
                    for j in range(2):
                        full(b, i * 2 + (SLOT_A + j), j, j, b * USE[j] + i + 9, yhi, ylo,
                             before={0: ((ya_hi, n8 * 2 + 14), (ya_lo, n8 * 2 + 14)),
                                     KT - 1: ((ya_hi, n8 * 2 + 16), (ya_lo, n8 * 2 + 16))} if j == 0 else ())
                with pe.Fori(0, 3) as g:
                    gb_pair(g)
                    xb_pair(None, g, b * USE[0] + g * 2 + 13)
                    project(g, b * USE[0] + g * 2 + 14)
                gb_pair(3)
                project(3, win_use(b, 3))
                with pe.Fori(0, 4) as i:
                    for j in range(2):
                        full(b, i * 2 + (SLOT_B + j), j, 2 + j, b * USE[2 + j] + i + (12 + j), yhi, ylo,
                             before={KT - 2: ((drained[0], b * USE[0] + 21),),
                                     KT - 1: ((drained[1], b * USE[1] + 21),)} if j == 0 else ())
                with pe.Fori(0, 4) as i:
                    for j in range(2):
                        full(b, i * 2 + (SLOT_O + j), j, j, b * USE[j] + i + 20, xhi, xlo,
                             before={0: ((m_hi, n8 + 7), (m_lo, n8 + 7)),
                                     KT - 1: ((m_hi, n8 + 8), (m_lo, n8 + 8))} if j == 0 else ())
                def gate_tile(i):
                    full(b, i * 6 + SLOT_MLP, 0, 0, mlp_use(b, 0, i), yhi, ylo,
                         before={KT - 1: ((x1_hi, n8 + 8), (x1_lo, n8 + 8))})

                def hidden_and_down(i):
                    full(b, i * 6 + (SLOT_MLP + 1), 1, 1, mlp_use(b, 1, i), yhi, ylo)
                    full(b, i * 6 + (SLOT_MLP + 2), 0, 2, mlp_use(b, 2, i), yhi, ylo)
                    full(b, i * 6 + (SLOT_MLP + 3), 1, 3, mlp_use(b, 3, i), yhi, ylo)
                    h = b * FT + i * 2
                    order = [(m, k) for k in range(2) for m in range(4)] + [(m, k) for m in range(4, 8) for k in range(2)]
                    for m, k in order:
                        par = m // 4
                        if k == 0:
                            if m % 4 == 0:
                                pe.wait_ge(main_split, b * NSLOT + i * 6 + (SLOT_MLP + 4 + par + 3))
                            if m == 0:
                                pe.wait_ge(h_hi, h + 1)
                                pe.wait_ge(h_lo, h + 1)
                            pe.wait_ge(drained[m % 4], mlp_use(b, m % 4, i) + (2 + par))
                        if (m, k) == (0, 1):
                            pe.wait_ge(h_hi, h + 2)
                            pe.wait_ge(h_lo, h + 2)
                        w = 2 * (m % 4) + k
                        mm = product(m % 4, [(whi[:, par, w], wlo[:, par, w], xhi[:, k, :], xlo[:, k, :])], CW,
                                     k == 0, k == 1, main_begun if (m % 4, k) == (0, 0) else None)
                        if k == 1:
                            mm.then_inc(ready, 1)

                pe.wait_ge(x1_hi, n8 + 7)
                pe.wait_ge(x1_lo, n8 + 7)
                gate_tile(0)
                pe.wait_ge(q2_sum, n8 + 8)
                norm_sum(6, b * USE[3] + 17)
                with pe.Fori(0, PAIRS - 1) as i:
                    hidden_and_down(i)
                    gate_tile(i + 1)
                hidden_and_down(PAIRS - 1)
                if not last:
                    first_xa(b + 1, -1)
                pe.wait_ge(q3_sum, n8 + 8)
                norm_sum(6, b * USE[3] + (51 if last else 52))

            pe.wait_ge(setup, 1)
            first_xa(0, 0)
            with pe.Fori(0, NB - 1) as b:
                block_products(b, False)
            block_products(NB - 1, True)

        @block.scalar
        def _(act):
            def load_x(b, k, j):
                act.dma_start(xin[:, j, :], dx[b, k]).then_inc(x_in[j], 16)

            def gained(b, pos):
                k, j = XORDER[pos], pos % 2
                act.wait_ge(x_in[j], (b * 8 + (pos // 2 - 3)) * 16)
                if pos == 6:
                    act.wait_ge(ready, b * TILES - 1)
                nc.scalar.activation(xhi[:, k, :], xin[:, j, :], ACT.Copy, scale=cst[:, G1, bass.ds(k, 1)]).then_inc(xg_hi, 1)

            def square_x(pos):
                nc.scalar.activation(tmp[:, 4 + pos % 2, 0:B], xin[:, pos % 2, :], ACT.Square).then_inc(x_sq, 1)

            def first_inputs():
                for pos in range(KT):
                    k = XORDER[pos]
                    act.wait_ge(x0_in[pos], 16)
                    nc.scalar.activation(xhi[:, k, :], main[:, k, :], ACT.Copy, scale=cst[:, G1, bass.ds(k, 1)]).then_inc(xg_hi, 1)
                    if pos >= 2:
                        act.wait_ge(q1_sum, pos - 1)
                    nc.scalar.activation(tmp[:, 4 + pos % 2, 0:B], main[:, k, :], ACT.Square).then_inc(x_sq, 1)

            def root(r, tile):
                act.wait_ge(ready, tile + 1)
                nc.scalar.activation(two(rstd[:, r, :]), bank(3, 0, CW), ACT.Sqrt, bias=epsc[:, 0:1], scale=1.0 / D).then_inc(drained[3], 1)

            def conv(b, h, j, use):
                n = b * 8 + h + 1
                act.wait_ge(drained[j], use + 2)
                act.nop(nofuse=True)
                nc.scalar.activation(gate[:, h, :], tbuf[:, j, 3:3 + TC], ACT.Identity,
                                     bias=cst[:, CB, bass.ds(h, 1)], scale=cst[:, CW0 + 3, bass.ds(h, 1)]).then_inc(tap3, 1)
                act.wait_ge(tap, n * 3)
                act.nop(nofuse=True)
                nc.scalar.activation(yhi[:, h, :], gate[:, h, :], ACT.Copy).then_inc(c_hi, 1)

            def gates(b, h, j, prev=False, free=False):
                n, t = b * 8 + h + 1, tile_ga(b, h)
                tr, ti, ta, tq = (tmp[:, 4 * j + v, 0:TC] for v in range(4))
                if free:
                    act.wait_ge(ya_lo, (n - 2) * 2)
                    act.nop(nofuse=True)
                act.wait_ge(ready, t + 2)
                act.nop(nofuse=True)
                nc.scalar.activation(two(tr), bank(2, 0, TC // 2), ACT.Sigmoid, bias=cst[:, BR, bass.ds(h, 1)]).then_inc(drained[2], 1)
                act.wait_ge(ready, t + 3)
                act.nop(nofuse=True)
                nc.scalar.activation(two(ti), bank(3, 0, TC // 2), ACT.Sigmoid, bias=cst[:, BI, bass.ds(h, 1)]).then_inc(drained[3], 1)
                act.wait_ge(drained[2], gate_use(b, 0, h) + 2)
                act.nop(nofuse=True)
                nc.scalar.activation(tq, tr, ACT.Tanh, scale=lac[:, 1, bass.ds(h, 1)]).then_inc(tanh_done, 1)
                nc.scalar.activation(ta, tr, ACT.Exp, scale=lac[:, 0, bass.ds(h, 1)]).then_inc(a_done, 1)
                if prev:
                    out_hi(b, h - 1, 1 - j)
                act.wait_ge(q_done, n)
                nc.scalar.activation(tq, tq, ACT.Sqrt).then_inc(mult_done, 1)

            def store_y(b, m):
                act.wait_ge(y_done, b * 8 + m + 1)
                act.nop(nofuse=True)
                act.dma_start(dy[b, m], main[:, m, :]).then_inc(y_stored, 16)

            def out_hi(b, h, j):
                tr = tmp[:, 4 * j, :]
                act.wait_ge(scan_s, b * 8 + h + 1)
                act.nop(nofuse=True)
                nc.scalar.activation(prompt(yhi[:, h, 0:B]), two(tr[:, 0:PTOK]), ACT.Copy).then_inc(ya_hi, 1)
                nc.scalar.activation(sample(yhi[:, h, 0:B]), two(tr[:, PTOK + 3:PTOK + 3 + SCOL]), ACT.Copy).then_inc(ya_hi, 1)

            def square_x2(b, m):
                act.wait_ge(drained[m % 4], mlp_use(b, m % 4, PAIRS - 1) + (3 + m // 4))
                nc.scalar.activation(tmp[:, 2 + m % 2, 0:B], main[:, m, :], ACT.Square).then_inc(x2_sq, 1)

            def hidden(b, i, j):
                f = b * FT + i * 2 + (j + 1)
                act.wait_ge(drained[2 * j], mlp_use(b, 2 * j, i) + 2)
                nc.scalar.activation(tmp[:, j, 0:B], tmp[:, j, 0:B], ACT.Silu).then_inc(silu, 1)
                act.wait_ge(drained[2 * j + 1], mlp_use(b, 2 * j + 1, i) + 2)
                nc.scalar.activation(xhi[:, j, :], tmp[:, 2 + j, 0:B], ACT.Copy).then_inc(h_hi, 1)

            def conv_rest(b):
                conv(b, 1, 1, b * USE[1])
                with act.Fori(0, 3) as i:
                    for j in range(2):
                        conv(b, i * 2 + (2 + j), j, b * USE[j] + i + 1)

            def heads(b, stores):
                gates(b, 0, 0)
                gates(b, 1, 1, prev=True)
                if stores:
                    store_y(b - 1, 0)
                with act.Fori(0, 3) as i:
                    for j in range(2):
                        gates(b, i * 2 + (2 + j), j, prev=True, free=True)
                        if stores:
                            store_y(b - 1, i * 2 + (1 + j))
                out_hi(b, 7, 1)
                if stores:
                    store_y(b - 1, 7)

            def window_hi(b, k):
                d = tmp[:, 4 * (k % 2) + 2, :]
                act.wait_ge(d_done, b * 8 + k + 1)
                nc.scalar.activation(prompt(yhi[:, k, 0:B]), two(d[:, PH:PH + PTOK]), ACT.Copy).then_inc(d_hi, 1)
                nc.scalar.activation(sample(yhi[:, k, 0:B]), two(d[:, 2 * PH + PTOK:TP]), ACT.Copy).then_inc(d_hi, 1)

            def block_act(b, last):
                n8 = b * 8
                with act.Fori(0, 4) as i:
                    for j in range(2):
                        h = i * 2 + j
                        act.wait_ge(drained[j], b * USE[j] + i + 6)
                        act.nop(nofuse=True)
                        nc.scalar.activation(gate[:, h, 0:B], gate[:, h, 0:B], ACT.Sigmoid).then_inc(sig_a, 1)
                act.wait_ge(ready, tile_a(b, KT))
                window_hi(b, 0)
                window_hi(b, 1)
                for g in range(4):
                    for j in range(2):
                        k = 2 * g + j
                        act.wait_ge(drained[2 + j], b * USE[2 + j] + g + 10 + j)
                        nc.scalar.activation(gate[:, k, 0:B], gate[:, k, 0:B], ACT.Sigmoid).then_inc(sig_b, 1)
                    if g < 3:
                        window_hi(b, 2 * g + 2)
                        window_hi(b, 2 * g + 3)
                    act.wait_ge(ready, tile_win(b, g, 1) + 1)
                    for j in range(2):
                        k = 2 * g + j
                        nc.scalar.activation(two(yhi[:, k, 0:B]), bank(j, 0, CW), ACT.Copy, scale=cst[:, PSC, bass.ds(k, 1)]).then_inc(yb_hi, 1)
                with act.Fori(0, 4) as i:
                    for j in range(2):
                        m = i * 2 + j
                        act.wait_ge(merged, n8 + m + 1)
                        act.nop(nofuse=True)
                        nc.scalar.activation(xhi[:, m, :], main[:, m, :], ACT.Copy).then_inc(m_hi, 1)

                def residual(m, i, j):
                    act.wait_ge(drained[j], b * USE[j] + i + 22)
                    act.nop(nofuse=True)
                    nc.scalar.activation(yhi[:, m, 0:B], main[:, m, :], ACT.Copy, scale=cst[:, G2, bass.ds(m, 1)]).then_inc(x1_hi, 1)
                    nc.scalar.activation(tmp[:, 4 + j, 0:B], main[:, m, :], ACT.Square).then_inc(x1_sq, 1)

                with act.Fori(0, 3) as i:
                    for j in range(2):
                        residual(i * 2 + j, i, j)
                        load_x(b, i * 2 + (2 + j), j)
                for j in range(2):
                    residual(6 + j, 3, j)
                    if not last:
                        load_x(b + 1, XORDER[j], j)
                root(1, tile_norm(b, 0))
                with act.Fori(0, PAIRS - 1) as i:
                    hidden(b, i, 0)
                    hidden(b, i, 1)
                if not last:
                    for pos in range(6):
                        gained(b + 1, pos)
                        square_x(pos)
                        act.wait_ge(q1_sum, n8 + 9 + pos)
                        load_x(b + 1, XORDER[pos + 2], pos % 2)
                hidden(b, PAIRS - 1, 0)
                hidden(b, PAIRS - 1, 1)
                for m in range(KT - 1):
                    square_x2(b, m)
                if not last:
                    gained(b + 1, 6)
                    gained(b + 1, 7)
                square_x2(b, KT - 1)
                if not last:
                    for pos in (6, 7):
                        square_x(pos)
                    for pos in (6, 7):
                        act.wait_ge(q1_sum, n8 + 9 + pos)
                        load_x(b + 1, pos - 6, pos % 2)
                    root(0, tile_norm(b, 1))
                    conv(b + 1, 0, 0, (b + 1) * USE[0])
                root(1, tile_norm(b, 2, last))

            for pos in (0, 2, 4, 6):
                act.dma_start(main[:, XORDER[pos], :], dx[0, XORDER[pos]]).then_inc(x0_in[pos], 16)
            act.wait_ge(setup, 1)
            act.wait_ge(consts_in, 16)
            first_inputs()
            load_x(0, 0, 0)
            load_x(0, 1, 1)
            act.wait_ge(lam_exp, 1)
            nc.scalar.activation(lac[:, 3, :], lac[:, 2, :], ACT.Exp, scale=-1.0).then_inc(lam_exp, 1)
            act.wait_ge(lam_done, 1)
            root(0, 1)
            conv(0, 0, 0, 0)
            conv_rest(0)
            heads(0, False)
            with act.Fori(0, NB - 1) as b:
                block_act(b, False)
                conv_rest(b + 1)
                heads(b + 1, True)
            block_act(NB - 1, True)
            for m in range(YV):
                act.wait_ge(y_last, m + 1)
                act.dma_start(dy[NB - 1, m], main[:, m, :]).then_inc(y_stored, 16)

        @block.vector
        def _(dve):
            V = nc.vector

            def gained(b, pos, src):
                k, n = XORDER[pos], b * 8 + pos + 1
                dve.wait_ge(xg_hi, n)
                V.scalar_tensor_tensor(xlo[:, k, :], src, cst[:, G1, bass.ds(k, 1)], xhi[:, k, :].bitcast(f32), MUL, SUB).then_inc(xg_lo, 1)

            def sum_x(b, pos):
                n = b * 8 + pos + 1
                dve.wait_ge(x_sq, n)
                dve.wait_ge(q1_sum, n - 1) if pos else dve.wait_ge(q1_zero, b + 1)
                V.tensor_tensor(tmp[:, 7, 0:B], tmp[:, 7, 0:B], tmp[:, 4 + pos % 2, 0:B], ADD).then_inc(q1_sum, 1)

            def invert(r, use, done):
                dve.wait_ge(drained[3], use + 2)
                V.reciprocal(rstd[:, r, :], rstd[:, r, :]).then_inc(done, 1)

            def conv_lo(b, h):
                dve.wait_ge(c_hi, b * 8 + h + 1)
                V.tensor_tensor(ylo[:, h, :], gate[:, h, :], yhi[:, h, :].bitcast(f32), SUB).then_inc(c_lo, 1)

            def conv(b, h, j, use, tile, prev=True):
                n, t = b * 8 + h + 1, tbuf[:, j, :]
                r2 = two(rstd[:, 0, :])
                V.tensor_copy(t[:, 0:3], state[:, h, S_CONV + 1:S_CONV + 4]).then_inc(xa_hist, 1)
                V.tensor_copy(t[:, PTOK + 3:PTOK + 6], state[:, h, S_CONV + 5:S_CONV + 8]).then_inc(xa_hist, 1)
                dve.wait_ge(ready, tile + 1)
                V.tensor_tensor(two(t[:, 3:3 + PTOK]), bank(j, 0, PC), r2[:, :, 0:PC], MUL).then_inc(xa_part, 1)
                V.tensor_tensor(two(t[:, PTOK + 6:PTOK + 6 + SCOL]), bank(j, PC, CW), r2[:, :, PC:CW], MUL).then_inc(drained[j], 1)
                if prev:
                    conv_lo(b, h - 1)
                dve.wait_ge(drained[j], use + 2)
                rows = t[:, PTOK - 1:PTOK - 1 + 28].rearrange("p (s n) -> p s n", s=2)[:, :, 0:4]
                V.tensor_copy(state[:, h, S_CONV:S_CONV + 8].rearrange("p (s n) -> p s n", s=2), rows).then_inc(xa_saved, 1)
                dve.wait_ge(tap3, n)
                for i, w in enumerate((2, 1, 0)):
                    if i:
                        dve.wait_ge(tap, (n - 1) * 3 + i)
                    V.scalar_tensor_tensor(gate[:, h, :], t[:, w:w + TC], cst[:, CW0 + w, bass.ds(h, 1)], gate[:, h, :], MUL, ADD).then_inc(tap, 1)

            def gates(b, h, j):
                n = b * 8 + h + 1
                tr, ti, ta, tq = (tmp[:, 4 * j + v, 0:TC] for v in range(4))
                dve.wait_ge(drained[3], gate_use(b, 1, h) + 2)
                V.tensor_tensor(ti, ti, gate[:, h, :], MUL).then_inc(ix_done, 1)
                dve.wait_ge(ix_done, n)
                dve.wait_ge(ready, tile_ga(b, h) + 1)
                V.tensor_tensor(two(gate[:, h, 0:B]), bank(j, 0, CW), two(rstd[:, 0, :]), MUL).then_inc(drained[j], 1)
                dve.wait_ge(a_done, n)
                V.tensor_tensor(tr, ta, ta, MUL).then_inc(a2_done, 1)
                dve.wait_ge(a2_done, n)
                V.scalar_tensor_tensor(tq, tr, 1.0, tq, ADD, MUL).then_inc(q_done, 1)

            def recur(b, h, j):
                n = b * 8 + h + 1
                tr, ti, ta, tq = (tmp[:, 4 * j + v, :] for v in range(4))
                dve.wait_ge(mult_done, n)
                V.tensor_scalar(tq[:, 0:1], tq[:, 0:1], fix[:, 64:65], fix[:, 65:66], MUL, ADD).then_inc(pos0, 1)
                dve.wait_ge(pos0, n)
                V.tensor_tensor(ti[:, 0:TC], tq[:, 0:TC], ti[:, 0:TC], MUL).then_inc(bt_done, 1)
                dve.wait_ge(bt_done, n)
                s = PTOK + 3
                V.tensor_tensor_scan(tr[:, 0:PTOK], ta[:, 0:PTOK], ti[:, 0:PTOK], state[:, h, S_LRU + 1:S_LRU + 2], MUL, ADD).then_inc(scan_p, 1)
                V.tensor_tensor_scan(tr[:, s:s + SCOL], ta[:, s:s + SCOL], ti[:, s:s + SCOL], state[:, h, S_LRU + 3:S_LRU + 4], MUL, ADD).then_inc(scan_s, 1)
                dve.wait_ge(scan_s, n)
                last2 = tr[:, PTOK - 2:PTOK - 2 + 28].rearrange("p (s n) -> p s n", s=2)[:, :, 0:2]
                V.tensor_copy(state[:, h, S_LRU:S_LRU + 4].rearrange("p (s n) -> p s n", s=2), last2).then_inc(h_saved, 1)

            def out_lo(b, h, j):
                tr = tmp[:, 4 * j, :]
                dve.wait_ge(ya_hi, (b * 8 + h + 1) * 2)
                V.tensor_tensor(prompt(ylo[:, h, 0:B]), two(tr[:, 0:PTOK]), prompt(yhi[:, h, 0:B]).bitcast(f32), SUB).then_inc(ya_lo, 1)
                V.tensor_tensor(sample(ylo[:, h, 0:B]), two(tr[:, PTOK + 3:PTOK + 3 + SCOL]), sample(yhi[:, h, 0:B]).bitcast(f32), SUB).then_inc(ya_lo, 1)

            def window(b, g, j):
                k = 2 * g + j
                n, t, w = b * 8 + k + 1, tbuf[:, j, :], WINDOWS[g]
                r2 = two(rstd[:, 0, :])
                V.tensor_copy(t[:, 0:PH], state[:, k, S_POOL + 1:S_POOL + 16]).then_inc(xb_hist, 1)
                V.tensor_copy(t[:, PTOK + PH:PTOK + 2 * PH], state[:, k, S_POOL + 17:S_POOL + 32]).then_inc(xb_hist, 1)
                dve.wait_ge(ready, tile_xb(b, g, j) + 1)
                V.tensor_tensor(two(t[:, PH:PH + PTOK]), bank(j, 0, PC), r2[:, :, 0:PC], MUL).then_inc(xb_part, 1)
                V.tensor_tensor(two(t[:, 2 * PH + PTOK:TP]), bank(j, PC, CW), r2[:, :, PC:CW], MUL).then_inc(drained[j], 1)
                dve.wait_ge(drained[j], xb_use(b, g) + 2)
                V.tensor_copy(state[:, k, S_POOL:S_POOL + 16], t[:, PTOK - 1:PTOK + 15]).then_inc(xb_saved, 1)
                V.tensor_copy(state[:, k, S_POOL + 16:S_POOL + 32], t[:, PTOK + 25:PTOK + 41]).then_inc(xb_saved, 1)
                src, span = t, 1
                steps = g + 1
                for q in range(steps):
                    out = tmp[:, 4 * j + q % 2, :]
                    if q:
                        dve.wait_ge(wsum, wsums(b, g, j) + q)
                    first = 2 * span - 1
                    V.tensor_tensor(out[:, first:TP], src[:, first:TP], src[:, first - span:TP - span], ADD).then_inc(wsum, 1)
                    src, span = out, 2 * span
                dve.wait_ge(wsum, wsums(b, g, j) + steps)
                V.tensor_tensor(src[:, PH:2 * PH], src[:, PH:2 * PH], fix[:, 16 * g:16 * g + PH], MUL).then_inc(wfix, 1)
                dve.wait_ge(wfix, n)
                d = tmp[:, 4 * j + 2, :]
                V.scalar_tensor_tensor(d[:, PH:TP], src[:, PH:TP], 1.0 / w, t[:, PH:TP], MUL, SUB).then_inc(d_done, 1)

            def window_lo(b, k):
                d = tmp[:, 4 * (k % 2) + 2, :]
                dve.wait_ge(d_hi, (b * 8 + k + 1) * 2)
                V.tensor_tensor(prompt(ylo[:, k, 0:B]), two(d[:, PH:PH + PTOK]), prompt(yhi[:, k, 0:B]).bitcast(f32), SUB).then_inc(d_lo, 1)
                V.tensor_tensor(sample(ylo[:, k, 0:B]), two(d[:, 2 * PH + PTOK:TP]), sample(yhi[:, k, 0:B]).bitcast(f32), SUB).then_inc(d_lo, 1)

            def hidden(b, i, j):
                f, r2 = b * FT + i * 2 + (j + 1), two(rstd[:, 1, :])
                t, h = tmp[:, j, 0:B], tmp[:, 2 + j, 0:B]
                dve.wait_ge(ready, tile_mlp(b, i) + (1 + 2 * j))
                V.tensor_tensor(two(t), bank(2 * j, 0, CW), r2, MUL).then_inc(drained[2 * j], 1)
                dve.wait_ge(silu, f)
                V.tensor_tensor(t, t, rstd[:, 1, :], MUL).then_inc(sr_done, 1)
                dve.wait_ge(ready, tile_mlp(b, i) + (2 + 2 * j))
                dve.wait_ge(sr_done, f)
                V.tensor_tensor(two(h), bank(2 * j + 1, 0, CW), two(t), MUL).then_inc(drained[2 * j + 1], 1)
                dve.wait_ge(h_hi, f)
                V.tensor_tensor(xlo[:, j, :], h, xhi[:, j, :].bitcast(f32), SUB).then_inc(h_lo, 1)

            def add_down(b, i, m):
                dve.wait_ge(ready, tile_mlp(b, i) + (5 + m))
                V.tensor_tensor(two(main[:, m, :]), bank(m % 4, 0, CW), two(main[:, m, :]), ADD).then_inc(drained[m % 4], 1)

            def square_sum(b, m):
                n = b * 8 + m + 1
                dve.wait_ge(x2_sq, n)
                dve.wait_ge(q3_sum, n - 1) if m else dve.wait_ge(q3_zero, b + 1)
                V.tensor_tensor(tmp[:, 6, 0:B], tmp[:, 6, 0:B], tmp[:, 2 + m % 2, 0:B], ADD).then_inc(q3_sum, 1)

            def conv_rest(b, invert_last):
                conv(b, 1, 1, b * USE[1], tile_xa(b, 1))
                if invert_last:
                    invert(1, b * USE[3], rstd3)
                with dve.Fori(0, 3) as i:
                    for j in range(2):
                        conv(b, i * 2 + (2 + j), j, b * USE[j] + i + 1, tile_xa(b, i * 2 + (2 + j)))
                conv_lo(b, 7)

            def heads(b):
                gates(b, 0, 0)

                def step(h, j):
                    recur(b, h - 1, 1 - j)
                    gates(b, h, j)
                    out_lo(b, h - 1, 1 - j)

                step(1, 1)
                with dve.Fori(0, 3) as i:
                    step(i * 2 + 2, 0)
                    step(i * 2 + 3, 1)
                recur(b, 7, 1)
                out_lo(b, 7, 1)

            def block_dve(b, last):
                n8 = b * 8
                window(b, 0, 0)
                window(b, 0, 1)
                dve.wait_ge(y_stored, b * (16 * KT) + 16)
                dve.nop(nofuse=True)
                with dve.Fori(0, 4) as i:
                    for j in range(2):
                        m = i * 2 + j
                        dve.wait_ge(sig_a, n8 + m + 1)
                        dve.wait_ge(ready, tile_a(b, m) + 1)
                        V.tensor_tensor(two(main[:, m, :]), bank(j, 0, CW), two(gate[:, m, 0:B]), MUL).then_inc(drained[j], 1)
                window_lo(b, 0)
                window_lo(b, 1)
                for g in range(4):
                    for j in range(2):
                        dve.wait_ge(ready, tile_gb(b, g, j) + 1)
                        V.tensor_tensor(two(gate[:, 2 * g + j, 0:B]), bank(2 + j, 0, CW), two(rstd[:, 0, :]), MUL).then_inc(drained[2 + j], 1)
                    if g < 3:
                        for j in range(2):
                            window(b, g + 1, j)
                            window_lo(b, 2 * g + 2 + j)
                    for j in range(2):
                        k = 2 * g + j
                        dve.wait_ge(yb_hi, n8 + k + 1)
                        V.scalar_tensor_tensor(two(ylo[:, k, 0:B]), bank(j, 0, CW), cst[:, PSC, bass.ds(k, 1)],
                                               two(yhi[:, k, 0:B]).bitcast(f32), MUL, SUB).then_inc(drained[j], 1)
                with dve.Fori(0, 4) as i:
                    for j in range(2):
                        m = i * 2 + j
                        dve.wait_ge(sig_b, n8 + m + 1)
                        dve.wait_ge(ready, tile_b(b, m) + 1)
                        V.tensor_tensor(two(tmp[:, j, 0:B]), bank(2 + j, 0, CW), two(gate[:, m, 0:B]), MUL).then_inc(drained[2 + j], 1)
                        dve.wait_ge(drained[2 + j], b * USE[2 + j] + i + (14 + j))
                        V.tensor_tensor(main[:, m, :], main[:, m, :], tmp[:, j, 0:B], ADD).then_inc(merged, 1)
                        dve.wait_ge(m_hi, n8 + m + 1)
                        V.tensor_tensor(xlo[:, m, :], main[:, m, :], xhi[:, m, :].bitcast(f32), SUB).then_inc(m_lo, 1)
                V.memset(tmp[:, 6, 0:B], 0.0).then_inc(q2_zero, 1)
                dve.wait_ge(q2_zero, b + 1)
                dve.nop(nofuse=True)
                with dve.Fori(0, 4) as i:
                    for j in range(2):
                        m = i * 2 + j
                        dve.wait_ge(x_in[j], (n8 + i + 1) * 16)
                        dve.wait_ge(ready, tile_o(b, m) + 1)
                        V.tensor_tensor(two(main[:, m, :]), bank(j, 0, CW), two(xin[:, j, :]), ADD).then_inc(drained[j], 1)
                        dve.wait_ge(x1_hi, n8 + m + 1)
                        V.scalar_tensor_tensor(ylo[:, m, 0:B], main[:, m, :], cst[:, G2, bass.ds(m, 1)], yhi[:, m, 0:B].bitcast(f32), MUL, SUB).then_inc(x1_lo, 1)
                        dve.wait_ge(x1_sq, n8 + m + 1)
                        V.tensor_tensor(tmp[:, 6, 0:B], tmp[:, 6, 0:B], tmp[:, 4 + j, 0:B], ADD).then_inc(q2_sum, 1)
                invert(1, b * USE[3] + 17, rstd2)
                dve.wait_ge(rstd2, b + 1)
                dve.nop(nofuse=True)
                with dve.Fori(0, PAIRS - 1) as i:
                    hidden(b, i, 0)
                    hidden(b, i, 1)
                    for m in range(KT):
                        add_down(b, i, m)
                if not last:
                    V.memset(tmp[:, 7, 0:B], 0.0).then_inc(q1_zero, 1)
                    for pos in range(6):
                        gained(b + 1, pos, xin[:, pos % 2, :])
                        sum_x(b + 1, pos)
                hidden(b, PAIRS - 1, 0)
                hidden(b, PAIRS - 1, 1)
                V.memset(tmp[:, 6, 0:B], 0.0).then_inc(q3_zero, 1)
                for m in range(KT):
                    add_down(b, PAIRS - 1, m)
                    if m:
                        square_sum(b, m - 1)
                if not last:
                    gained(b + 1, 6, xin[:, 0, :])
                    gained(b + 1, 7, xin[:, 1, :])
                square_sum(b, KT - 1)
                if not last:
                    sum_x(b + 1, 6)
                    sum_x(b + 1, 7)
                    V.memset(fix[:, 0:65], 1.0).then_inc(unfix, 1)
                    V.memset(fix[:, 65:66], 0.0).then_inc(unfix, 1)
                    invert(0, (b + 1) * USE[3] - 1, rstd1)
                    dve.wait_ge(rstd1, b + 2)
                    conv(b + 1, 0, 0, (b + 1) * USE[0], tile_xa(b + 1, -2), prev=False)

            V.memset(credit[:, 0:1], 0.0).then_inc(main_split, 2)
            V.memset(credit[:, 1:2], 0.0).then_inc(main_begun, 1)
            V.memset(credit[:, 2:3], 0.0).then_inc(side_split, 1)
            V.memset(credit[:, 3:4], 0.0).then_inc(y_stored, 16)
            for g in range(4):
                V.memset(credit[:, 4 + g:5 + g], 0.0).then_inc(drained[g], 1)
            V.memset(tbuf[:, :, 706:708], 0.0)
            V.memset(epsc[:], EPS)
            V.memset(ones[:], 1.0).then_inc(setup, 1)
            V.memset(tmp[:, 7, 0:B], 0.0).then_inc(q1_zero, 1)
            dve.wait_ge(consts_in, 16)
            for pos in range(KT):
                gained(0, pos, main[:, XORDER[pos], :])
                sum_x(0, pos)
            chain = [0]

            def link(ins):
                chain[0] += 1
                ins.then_inc(lam_chain, 1)
                dve.wait_ge(lam_chain, chain[0])

            lam = cst[:, LAM, :]
            link(V.tensor_scalar(lac[:, 2, :], lam, -1.0, None, MUL))
            V.tensor_tensor(lac[:, 2, :], lac[:, 2, :], lam, ALU.max).then_inc(lam_exp, 1)
            dve.wait_ge(lam_exp, 2)
            link(V.tensor_scalar(lac[:, 4, :], lac[:, 3, :], 2.0, None, ADD))
            link(V.reciprocal(lac[:, 4, :], lac[:, 4, :]))
            link(V.tensor_tensor(lac[:, 3, :], lac[:, 3, :], lac[:, 4, :], MUL))
            link(V.tensor_tensor(lac[:, 4, :], lac[:, 3, :], lac[:, 3, :], MUL))
            link(V.tensor_scalar(lac[:, 5, :], lac[:, 4, :], 1.0 / 17, None, MUL))
            for q in (15, 13, 11, 9, 7, 5, 3):
                link(V.scalar_tensor_tensor(lac[:, 5, :], lac[:, 5, :], 1.0 / q, lac[:, 4, :], ADD, MUL))
            link(V.scalar_tensor_tensor(lac[:, 5, :], lac[:, 5, :], 1.0, lac[:, 3, :], ADD, MUL))
            link(V.tensor_scalar(lac[:, 6, :], lam, 0.0, None, ALU.min))
            link(V.scalar_tensor_tensor(lac[:, 5, :], lac[:, 5, :], -2.0, lac[:, 6, :], MUL, ADD))
            link(V.tensor_scalar(lac[:, 0, :], lac[:, 5, :], LRU_C, None, MUL))
            V.tensor_scalar(lac[:, 1, :], lac[:, 5, :], -LRU_C, None, MUL).then_inc(lam_done, 1)
            invert(0, 0, rstd1)
            dve.wait_ge(rstd1, 1)
            dve.wait_ge(tables_in, 32)
            conv(0, 0, 0, 0, 0, prev=False)
            conv_rest(0, False)
            heads(0)
            with dve.Fori(0, NB - 1) as b:
                block_dve(b, False)
                conv_rest(b + 1, True)
                heads(b + 1)
            block_dve(NB - 1, True)
            invert(1, (NB - 1) * USE[3] + 51, rstd3)
            dve.wait_ge(rstd3, NB)
            for m in range(YV):
                V.scalar_tensor_tensor(main[:, m, :], main[:, m, :], cst[:, GF, bass.ds(m, 1)], rstd[:, 1, :], MUL, MUL).then_inc(y_last, 1)


def kernel(x_prompt, x_sample, state_conv, state_lru, state_pool, meta_tokens, norm1_g, w_in, conv_w, conv_b,
           lam, w_r, b_r, w_i, b_i, pool_w, pool_scale, w_br_a, w_br_b, w_out, norm2_g, w_gu, w_down, final_g):
    import concourse.bacc as _bacc
    from concourse.bass_utils import run_bass_kernel_spmd as _run

    A = np.asarray
    prompt = np.concatenate([A(meta_tokens), A(x_prompt)[0]], axis=0).reshape(NB, CH, PC, D)
    sample = np.concatenate([A(x_sample)[0], np.zeros((NB * STOK - DEC, D), np.float32)], axis=0).reshape(NB, STOK, D)
    sample = np.concatenate([sample, np.zeros((NB, 1, D), np.float32)], axis=1).reshape(NB, CH, SC, D)
    dx = np.concatenate([prompt, sample], axis=2).reshape(NB, B, KT, P).transpose(0, 2, 3, 1)

    def columns(w, c0, n):
        w = A(w)[:, c0:c0 + n * P]
        return w.reshape(KT, P, n, P).transpose(2, 1, 0, 3).reshape(n, P, KT * P)

    w_in, w_gu = A(w_in)[0], A(w_gu)[0]
    xb, gb = columns(w_in, D, KT), columns(w_in, 3 * D, KT)
    hg, hu = columns(w_gu, 0, FT), columns(w_gu, FF, FT)
    down = A(w_down)[0].reshape(PAIRS, 2, P, 2, 4, P).transpose(0, 3, 2, 4, 1, 5).reshape(PAIRS, 2, P, KT * P)
    slots = [columns(w_in, 0, KT), columns(w_in, 2 * D, KT), xb[0:2], columns(A(w_br_a)[0], 0, KT)]
    for g in range(4):
        slots += [gb[2 * g:2 * g + 2], xb[2 * g + 2:2 * g + 4]]
    slots += [columns(A(w_br_b)[0], 0, KT), columns(A(w_out)[0], 0, KT)]
    for i in range(PAIRS):
        slots += [hg[2 * i:2 * i + 1], hu[2 * i:2 * i + 1], hg[2 * i + 1:2 * i + 2], hu[2 * i + 1:2 * i + 2], down[i]]
    dwm = np.concatenate(slots, axis=0)
    ri = np.concatenate([A(w_r)[0], A(w_i)[0], np.zeros((KT, P, 2 * P), np.float32)], axis=2)
    pw = A(pool_w)[0].reshape(4, 2, P, 2, P).transpose(0, 2, 3, 1, 4).reshape(4, P, 4 * P)
    dws = np.concatenate([ri, pw], axis=0)
    rows = [A(norm1_g), A(conv_w)[0], A(conv_b), A(b_r), A(b_i), A(lam), A(pool_scale), A(norm2_g), A(final_g)[None]]
    dcst = np.concatenate(rows, axis=0).reshape(NCST, KT, P).transpose(2, 0, 1)
    fix = np.ones((P, 66), np.float32)
    for g, w in enumerate(WINDOWS):
        for t in range(w - 1):
            fix[:, 16 * g + t] = w / (t + 1)
    fix[:, 64] = 0.0
    st0 = np.zeros((P, KT, NST), np.float32)
    st0[:, :, S_CONV + 5:S_CONV + 8] = A(state_conv)[0, 0].reshape(3, KT, P).transpose(2, 1, 0)
    st0[:, :, S_LRU + 3] = A(state_lru)[0, 0].reshape(KT, P).transpose(1, 0)
    st0[:, :, S_POOL + 17:S_POOL + 32] = A(state_pool)[0, 0].reshape(PH, KT, P).transpose(2, 1, 0)

    nc = _bacc.Bacc("TRN2", target_bir_lowering=False, num_devices=1)
    arrays = {"dx": dx, "dwm": dwm, "dws": dws, "dcst": dcst, "dfix": fix, "dst0": st0}
    arrays = {k: np.ascontiguousarray(v) for k, v in arrays.items()}
    ins = [nc.dram_tensor(k, v.shape, mybir.dt.float32, kind="ExternalInput").ap() for k, v in arrays.items()]
    dy = nc.dram_tensor("dy", (NB, KT, P, B), mybir.dt.float32, kind="ExternalOutput").ap()
    dst = nc.dram_tensor("dst", (P, KT, NST), mybir.dt.float32, kind="ExternalOutput").ap()
    build(nc, *ins, dy, dst)
    r = _run(nc, [arrays], core_ids=[0]).results[0]

    y = A(r["dy"]).transpose(0, 3, 1, 2).reshape(NB, CH, CW, D)
    yp = y[:, :, 0:PC].reshape(1, SEQ + META, D)[:, META:]
    ys = y[:, :, PC:CW].reshape(NB, SCOL, D)[:, 0:STOK].reshape(1, NB * STOK, D)[:, 0:DEC]
    st = A(r["dst"]).transpose(2, 1, 0).reshape(NST, D)

    def rows_of(first, n):
        return np.ascontiguousarray(st[first:first + n])[None, None]

    return (np.ascontiguousarray(yp), np.ascontiguousarray(ys),
            rows_of(S_CONV + 1, 3), rows_of(S_LRU + 1, 1)[:, :, 0], rows_of(S_POOL + 1, PH),
            rows_of(S_CONV + 4, 3), rows_of(S_LRU + 2, 1)[:, :, 0], rows_of(S_POOL + 16, PH))
```
